# Optimizing a Trainium2 kernel written in Bass

```python
import jax, jax.numpy as jnp
from jax import lax
import numpy as np

D_MODEL = 1024
BATCH = 1
SEQ = 256
DEPTH = 2

N_MIXERS = 2
N_A_LAYERS = (DEPTH + 1) // 2
N_B_LAYERS = DEPTH // 2
RMS_EPS = 1e-6

RWKV_HEAD = 64
RWKV_HEADS = D_MODEL // RWKV_HEAD
LORA_DECAY = 64
LORA_AAA = 64
LORA_GATE = 160
RWKV_GN_EPS = 64e-5
N_SHIFT = 6

RET_HEADS = 4
RET_QK = D_MODEL // RET_HEADS
RET_V = 2 * RET_QK
RET_CHUNK = 128
ROPE_BASE = 10000.0

D_FF = 2816
N_EXPERTS = 8
TOP_K = 2
D_FF_EXPERT = 3584

kernel_name = "hybrid_rwkv7_retnet_moe"

def rmsnorm(x, g):
    xf = x.astype(jnp.float32)
    y = xf * lax.rsqrt(jnp.mean(xf * xf, axis=-1, keepdims=True) + RMS_EPS)
    return (y * g.astype(jnp.float32)).astype(x.dtype)

def token_shift(x):
    return jnp.pad(x, ((0, 0), (1, 0), (0, 0)))[:, :-1]

def rwkv7_time_mix(h, mu, wr, wk, wv, wo, w0, w1, w2, a0, a1, a2, g1, g2,
                   k_k, k_a, r_k, gn_w, gn_b):
    B, T, D = h.shape
    H, N = RWKV_HEADS, RWKV_HEAD
    f32 = jnp.float32
    dx = token_shift(h) - h
    xr = h + dx * mu[0]
    xw = h + dx * mu[1]
    xk = h + dx * mu[2]
    xv = h + dx * mu[3]
    xa = h + dx * mu[4]
    xg = h + dx * mu[5]
    r = xr @ wr
    k = xk @ wk
    v = xv @ wv
    w = -jax.nn.softplus(-(w0 + jnp.tanh(xw @ w1) @ w2)) - 0.5
    a = jax.nn.sigmoid(a0 + (xa @ a1) @ a2)
    g = jax.nn.sigmoid(xg @ g1) @ g2

    kk = (k * k_k).reshape(B, T, H, N).astype(f32)
    kk = kk / jnp.maximum(jnp.sqrt(jnp.sum(kk * kk, axis=-1, keepdims=True)), 1e-12)
    k = k * (1.0 + (a - 1.0) * k_a)

    def heads_tm(t):
        return t.astype(f32).reshape(B, T, H, N).transpose(1, 0, 2, 3)

    decay = jnp.exp(-jnp.exp(w.astype(f32)))
    a_h = heads_tm(a)
    kk_t = kk.transpose(1, 0, 2, 3)
    xs = (heads_tm(r), heads_tm(decay), heads_tm(k), heads_tm(v), -kk_t, kk_t * a_h)

    def step(S, inp):
        r_t, d_t, k_t, v_t, aa_t, bb_t = inp
        sa = jnp.einsum('bhvk,bhk->bhv', S, aa_t)
        S = S * d_t[:, :, None, :] + sa[..., :, None] * bb_t[..., None, :] \
            + v_t[..., :, None] * k_t[..., None, :]
        y = jnp.einsum('bhvk,bhk->bhv', S, r_t)
        return S, y

    S0 = jnp.zeros((B, H, N, N), f32)
    _, y = lax.scan(step, S0, xs)
    y = y.transpose(1, 0, 2, 3)

    mean = jnp.mean(y, axis=-1, keepdims=True)
    var = jnp.mean(jnp.square(y - mean), axis=-1, keepdims=True)
    y = ((y - mean) * lax.rsqrt(var + RWKV_GN_EPS)).reshape(B, T, D)
    y = y * gn_w.astype(f32) + gn_b.astype(f32)
    rh = r.astype(f32).reshape(B, T, H, N)
    kh = k.astype(f32).reshape(B, T, H, N)
    vh = v.astype(f32).reshape(B, T, H, N)
    bonus = jnp.sum(rh * kh * r_k.astype(f32), axis=-1, keepdims=True) * vh
    y = y + bonus.reshape(B, T, D)
    return ((y.astype(h.dtype) * g) @ wo).astype(h.dtype)

def rotate_every_two(t):
    t1 = t[..., ::2]
    t2 = t[..., 1::2]
    return jnp.stack((-t2, t1), axis=-1).reshape(t.shape)

def retention_rotation(t):
    T = t.shape[1]
    angle = 1.0 / (ROPE_BASE ** jnp.linspace(0.0, 1.0, RET_QK // 2, dtype=jnp.float32))
    angle = jnp.repeat(angle, 2)
    pos = jnp.arange(T, dtype=jnp.float32)
    ang = pos[:, None] * angle[None, :]
    sin = jnp.sin(ang)[None, :, None, :]
    cos = jnp.cos(ang)[None, :, None, :]
    return t * cos + rotate_every_two(t) * sin

def retention_mix(h, wq, wk, wv, wg, wo):
    B, T, D = h.shape
    H, dk, dv, C = RET_HEADS, RET_QK, RET_V, RET_CHUNK
    NC = T // C
    f32 = jnp.float32
    q = (h @ wq).astype(f32).reshape(B, T, H, dk)
    k = (h @ wk).astype(f32).reshape(B, T, H, dk) * (dk ** -0.5)
    v = (h @ wv).astype(f32).reshape(B, T, H, dv)
    g = h @ wg
    q = retention_rotation(q)
    k = retention_rotation(k)

    lg = jnp.log(1.0 - 2.0 ** (-5.0 - jnp.arange(H, dtype=f32)))
    n = jnp.arange(C, dtype=f32)
    diff = n[:, None] - n[None, :]
    intra = jnp.where(diff >= 0, jnp.exp(lg[:, None, None] * jnp.maximum(diff, 0.0)), 0.0)
    q_decay = jnp.exp(lg[:, None] * (n[None, :] + 1.0))
    k_decay = jnp.exp(lg[:, None] * (C - 1.0 - n[None, :]))
    chunk_decay = jnp.exp(lg * C)

    def chunks(t):
        return t.reshape(B, NC, C, H, t.shape[-1]).transpose(1, 0, 3, 2, 4)

    def step(R, inp):
        qc, kc, vc = inp
        s = jnp.einsum('bhcd,bhmd->bhcm', qc, kc) * intra[None]
        o = jnp.einsum('bhcm,bhme->bhce', s, vc) \
            + jnp.einsum('bhcd,bhde->bhce', qc, R) * q_decay[None, :, :, None]
        R = R * chunk_decay[None, :, None, None] \
            + jnp.einsum('bhmd,bhme->bhde', kc * k_decay[None, :, :, None], vc)
        return R, o

    R0 = jnp.zeros((B, H, dk, dv), f32)
    _, o = lax.scan(step, R0, (chunks(q), chunks(k), chunks(v)))
    o = o.transpose(1, 0, 3, 2, 4).reshape(B, T, H, dv)
    o = o * lax.rsqrt(jnp.mean(o * o, axis=-1, keepdims=True) + RMS_EPS)
    o = o.reshape(B, T, H * dv).astype(h.dtype)
    return ((jax.nn.silu(g) * o) @ wo).astype(h.dtype)

def swiglu(x, w1, w3, w2):
    return (jax.nn.silu(x @ w1) * (x @ w3)) @ w2

def moe_swiglu(h, router, w1, w3, w2):
    B, T, D = h.shape
    xt = h.reshape(B * T, D)
    logits = (xt @ router).astype(jnp.float32)
    top_val, top_idx = lax.top_k(logits, TOP_K)
    gates = jax.nn.softmax(top_val, axis=-1)
    combine = jnp.sum(jax.nn.one_hot(top_idx, N_EXPERTS, dtype=jnp.float32) * gates[..., None], axis=1)
    out = jnp.zeros((B * T, D), jnp.float32)
    for e in range(N_EXPERTS):
        out = out + combine[:, e:e + 1] * swiglu(xt, w1[e], w3[e], w2[e]).astype(jnp.float32)
    return out.astype(h.dtype).reshape(B, T, D)

def setup_inputs(seed: int = 0) -> dict:
    key = jax.random.key(seed)
    ks = iter(jax.random.split(key, 48))
    D = D_MODEL
    NA, NB = N_A_LAYERS, N_B_LAYERS
    H, N = RWKV_HEADS, RWKV_HEAD

    def nrm(shape, scale):
        return jax.random.normal(next(ks), shape, jnp.float32) * scale

    def uni(shape, lo, hi):
        return jax.random.uniform(next(ks), shape, jnp.float32, lo, hi)

    inp = {}
    inp["x"] = nrm((BATCH, SEQ, D), 1.0)
    inp["norm_mix"] = 1.0 + nrm((DEPTH, D), 0.02)
    inp["norm_ffn"] = 1.0 + nrm((DEPTH, D), 0.02)
    inp["norm_final"] = 1.0 + nrm((D,), 0.02)
    inp["a_mu"] = uni((NA, N_SHIFT, D), 0.0, 1.0)
    inp["a_wr"] = nrm((NA, D, D), D ** -0.5)
    inp["a_wk"] = nrm((NA, D, D), D ** -0.5)
    inp["a_wv"] = nrm((NA, D, D), D ** -0.5)
    inp["a_wo"] = nrm((NA, D, D), D ** -0.5)
    inp["a_w0"] = uni((NA, D), -6.0, 1.0)
    inp["a_w1"] = nrm((NA, D, LORA_DECAY), D ** -0.5)
    inp["a_w2"] = nrm((NA, LORA_DECAY, D), 0.1 * LORA_DECAY ** -0.5)
    inp["a_a0"] = nrm((NA, D), 0.1)
    inp["a_a1"] = nrm((NA, D, LORA_AAA), D ** -0.5)
    inp["a_a2"] = nrm((NA, LORA_AAA, D), 0.1 * LORA_AAA ** -0.5)
    inp["a_g1"] = nrm((NA, D, LORA_GATE), D ** -0.5)
    inp["a_g2"] = nrm((NA, LORA_GATE, D), LORA_GATE ** -0.5)
    inp["a_kk"] = 0.85 + nrm((NA, D), 0.05)
    inp["a_ka"] = 1.0 + nrm((NA, D), 0.05)
    inp["a_rk"] = nrm((NA, H, N), 0.1)
    inp["a_gn_w"] = 1.0 + nrm((NA, D), 0.02)
    inp["a_gn_b"] = nrm((NA, D), 0.02)
    inp["b_wq"] = nrm((NB, D, RET_HEADS * RET_QK), D ** -0.5)
    inp["b_wk"] = nrm((NB, D, RET_HEADS * RET_QK), D ** -0.5)
    inp["b_wv"] = nrm((NB, D, RET_HEADS * RET_V), D ** -0.5)
    inp["b_wg"] = nrm((NB, D, RET_HEADS * RET_V), D ** -0.5)
    inp["b_wo"] = nrm((NB, RET_HEADS * RET_V, D), (RET_HEADS * RET_V) ** -0.5)
    inp["f_w1"] = nrm((NA, D, D_FF), D ** -0.5)
    inp["f_w3"] = nrm((NA, D, D_FF), D ** -0.5)
    inp["f_w2"] = nrm((NA, D_FF, D), D_FF ** -0.5)
    inp["m_router"] = nrm((NB, D, N_EXPERTS), D ** -0.5)
    inp["m_w1"] = nrm((NB, N_EXPERTS, D, D_FF_EXPERT), D ** -0.5)
    inp["m_w3"] = nrm((NB, N_EXPERTS, D, D_FF_EXPERT), D ** -0.5)
    inp["m_w2"] = nrm((NB, N_EXPERTS, D_FF_EXPERT, D), D_FF_EXPERT ** -0.5)
    return inp

def reference(x, norm_mix, norm_ffn, norm_final,
              a_mu, a_wr, a_wk, a_wv, a_wo, a_w0, a_w1, a_w2, a_a0, a_a1, a_a2,
              a_g1, a_g2, a_kk, a_ka, a_rk, a_gn_w, a_gn_b,
              b_wq, b_wk, b_wv, b_wg, b_wo,
              f_w1, f_w3, f_w2,
              m_router, m_w1, m_w3, m_w2):
    h = x
    for i in range(DEPTH):
        j = i // N_MIXERS
        u = rmsnorm(h, norm_mix[i])
        if i % N_MIXERS == 0:
            h = h + rwkv7_time_mix(u, a_mu[j], a_wr[j], a_wk[j], a_wv[j], a_wo[j],
                                   a_w0[j], a_w1[j], a_w2[j], a_a0[j], a_a1[j], a_a2[j],
                                   a_g1[j], a_g2[j], a_kk[j], a_ka[j], a_rk[j],
                                   a_gn_w[j], a_gn_b[j])
        else:
            h = h + retention_mix(u, b_wq[j], b_wk[j], b_wv[j], b_wg[j], b_wo[j])
        u = rmsnorm(h, norm_ffn[i])
        c = i // 2
        if i % 2 == 0:
            h = h + swiglu(u, f_w1[c], f_w3[c], f_w2[c]).astype(h.dtype)
        else:
            h = h + moe_swiglu(u, m_router[c], m_w1[c], m_w3[c], m_w2[c])
    return rmsnorm(h, norm_final)


_drawn_inputs = setup_inputs


def setup_inputs(seed=0):
    import zlib

    import numpy as np

    out = dict(_drawn_inputs(seed))
    spreads = {}
    factors = {'norm_final': 2.992, 'a_w1': 4.64, 'a_w2': 4.962}
    for name, (base, spread) in spreads.items():
        noise = np.random.default_rng([zlib.crc32(name.encode()), seed]).standard_normal(out[name].shape)
        drawn = base * np.exp(spread * noise) if base else spread * noise
        out[name] = __import__('jax').numpy.asarray(drawn.astype(out[name].dtype))
    for name, factor in factors.items():
        out[name] = (out[name] * factor).astype(out[name].dtype)
    return out
```

```python
import math
from contextlib import ExitStack

import numpy as np
import concourse.bass as bass
from concourse import mybir

F32 = mybir.dt.float32
I32 = mybir.dt.int32
ALU = mybir.AluOpType
ACT = mybir.ActivationFunctionType
AX = mybir.AxisListType

P = 128
D = 1024
T = 256
KT = D // P
TT = T // P
EPS = 1e-6
GN_EPS = 64e-5
NH, HN = 16, 64
NP = NH // 2
CH = 64
NC = T // CH
LEVELS = 6
FF = 2816
FT = FF // P
RH, RK, RV = 4, 256, 512
NE = 8
FE = 3584
FJ = FE // 512
SLOT = 4096
RING = 7
R_SLOTS = 10
F_SLOTS = 17
B_SLOTS = 16
E_SLOTS = 3 * FJ
PRE = F_SLOTS + B_SLOTS
EXTRA = 3
assert E_SLOTS % RING == 0 and PRE % RING == 5

C_ID, C_ONE, C_TRI, C_IOTA, C_TIE, C_EIDX = 0, 128, 256, 384, 512, 576
C_COLS = 592
(V_NM0, V_NF0, V_NM1, V_NF1, V_MU, V_W0, V_A0, V_KK, V_KA, V_RK) = (0, 1, 2, 3, 4, 10, 11, 12, 13, 14)
P_ROUTER = 15 * KT
P_COLS = P_ROUTER + KT * NE
Q_BO, Q_MASK, Q_SEL, Q_ML, Q_MU, Q_EYE, Q_LEV = 0, 128, 256, 258, 322, 386, 450
Q_COLS = Q_LEV + 2 * LEVELS * 64


def const_tables():
    i = np.arange(P)
    c = np.zeros((P, C_COLS), np.float32)
    c[:, C_ID:C_ID + P] = np.eye(P)
    c[:, C_ONE:C_ONE + P] = 1
    c[:, C_TRI:C_TRI + P] = i[:, None] <= i[None, :]
    c[:, C_IOTA:C_IOTA + P] = i[None, :] + 1
    e = np.arange(NE)
    c[:, C_TIE:C_TIE + 64] = (e[None, :] < e[:, None]).reshape(-1)
    c[:, C_EIDX:C_EIDX + NE] = e
    q = np.zeros((P, Q_COLS), np.float32)
    q[:, Q_BO:Q_BO + P] = (i[:, None] // 64) == (i[None, :] // 64)
    s, t = i[:, None] % 64, i[None, :] % 64
    q[:, Q_MASK:Q_MASK + P] = np.where(i[None, :] < 64, s < t, s <= t)
    q[:, Q_SEL:Q_SEL + 2] = (i[:, None] // 64) == np.arange(2)[None, :]
    r, k = i[:, None] % 64, np.arange(64)[None, :]
    q[:, Q_ML:Q_ML + 64] = r > k
    q[:, Q_MU:Q_MU + 64] = r < k
    q[:, Q_EYE:Q_EYE + 64] = r == k
    for lv in range(LEVELS):
        b = 2 << lv
        same = (r // b) == (k // b)
        low = same & (r % b >= b // 2) & (k % b < b // 2)
        up = same & (k % b >= b // 2) & (r % b < b // 2)
        q[:, Q_LEV + 128 * lv:Q_LEV + 128 * lv + 64] = low
        q[:, Q_LEV + 128 * lv + 64:Q_LEV + 128 * lv + 128] = up
    f32 = np.float32
    angle = (f32(1.0) / (f32(10000.0) ** np.linspace(0, 1, RK // 2, dtype=f32))).astype(f32)
    ang = (angle[:, None] * np.arange(T, dtype=f32)[None, :]).astype(f32)
    tab = np.zeros((P, 2 * T + RH * 384), f32)
    tab[:, 0:T] = np.cos(ang.astype(np.float64))
    tab[:, T:2 * T] = np.sin(ang.astype(np.float64))
    for h in range(RH):
        lg = math.log(1.0 - 2.0 ** (-5.0 - h))
        for m0, c0, n, at in ((0, 0, 256, 0), (128, 128, 128, 256)):
            dif = (c0 + np.arange(n))[None, :] - (m0 + i)[:, None]
            tab[:, 2 * T + 384 * h + at:2 * T + 384 * h + at + n] = np.where(
                dif >= 0, np.exp(lg * np.maximum(dif, 0)) * RK ** -0.5, 0)
    return c, q, tab


def build(nc, x, consts, qconsts, tabs, params, rows, rstream, pstream, mstream, out):
    ctx = ExitStack()
    with ctx:
        def sb(name, cols, dt=F32):
            return ctx.enter_context(nc.sbuf_tensor(name, [P, cols], dt))

        def sem(name):
            return ctx.enter_context(nc.semaphore(name))

        ring = sb("ring", RING * SLOT)
        work = sb("work", 10 * 2048)
        h = sb("h", TT * D)
        cst = sb("cst", C_COLS)
        par = sb("par", P_COLS)
        small = sb("small", 256)
        route = sb("route", 384)
        itab = sb("itab", 8, I32)
        ps = ctx.enter_context(nc.psum_tensor("ps", [P, 8, 512], F32))

        def slot(p):
            return ring[:, p * SLOT:(p + 1) * SLOT]

        def vec(v, k):
            return par[:, v * KT + k:v * KT + k + 1]

        hv = h[:, :].rearrange("p (t d) -> p t d", t=TT)
        ident = cst[:, C_ID:C_ID + P]
        ones = cst[:, C_ONE:C_ONE + P]

        def blk(n, count=1):
            if n < 8:
                return ring[:, 3 * SLOT + n * 2048:3 * SLOT + (n + count) * 2048]
            return work[:, (n - 8) * 2048:(n - 8 + count) * 2048]

        def fm(a):
            return a.rearrange("p (k t) -> p k t", k=KT)

        uT_r, dxT = fm(blk(0)), fm(blk(1))
        mix = [fm(blk(2)), fm(blk(3))]
        kT, rT, aT = blk(4), blk(5), blk(6)
        dT, d1T, gT, giT = blk(7), blk(8), blk(11), blk(7)
        sqT, kkT, kmT = blk(8), blk(9), blk(10)
        BK = blk(0, 2).rearrange("p (n c x t) -> p n c x t", n=NP, c=NC, x=2)
        BKT = blk(2, 2).rearrange("p (n c k) -> p n c k", n=NP, c=NC)
        BKh = blk(8, 2).rearrange("p (n c k) -> p n c k", n=NP, c=NC)
        UV = blk(12, 2).rearrange("p (c h v) -> p c h v", c=NC, h=NH)
        gtok = blk(14).rearrange("p (t d) -> p t d", t=TT)
        vtok_r = blk(15).rearrange("p (t d) -> p t d", t=TT)
        AR = blk(16, 2).rearrange("p (n c x t) -> p n c x t", n=NP, c=NC, x=2)
        ygT = fm(blk(16))
        Qm = [blk(4 + i).rearrange("p (h t) -> p h t", h=NH) for i in range(2)]
        sets = []
        for a, b, c in ((6, 7, 11), (8, 9, 10)):
            bd = [v.rearrange("p (x n s) -> p x n s", x=2, n=NP) for v in (blk(a), blk(b))]
            st = blk(c).rearrange("p (x n s) -> p x n s", x=4, n=NP)
            sets.append(dict(bdM=bd[0][:, 0], bdMT=bd[0][:, 1], bdT=bd[1][:, 0], bdTT=bd[1][:, 1],
                             T=st[:, 0], TT=st[:, 1], W=st[:, 2], WT=st[:, 3], bds=(blk(a), blk(b))))
        qc = ring[:, 2 * SLOT:2 * SLOT + Q_COLS]
        gnw = ring[:, 2 * SLOT + 1280:2 * SLOT + 2304]
        gnb = ring[:, 2 * SLOT + 2304:2 * SLOT + 3328]
        Xst = ring[:, 2 * SLOT + 3328:2 * SLOT + 3840].rearrange("p (n v) -> p n v", n=NP)
        assert Q_COLS <= 1280
        yS = ring[:, SLOT:SLOT + 2048].rearrange("p (t h v) -> p t h v", t=TT, h=NH)
        bdS = [ring[:, SLOT + 2048 + 1024 * i:SLOT + 3072 + 1024 * i].rearrange(
            "p (n v) -> p n v", n=NP) for i in range(2)]
        lora_sb = blk(16)
        lor, sg1, sg2 = lora_sb[:, 0:T], lora_sb[:, T:2 * T], lora_sb[0:32, 2 * T:3 * T]
        gC = small[:, 64:96]
        bon = small[:, 96:128].rearrange("p (t h) -> p t h", t=TT)
        gsum = small[:, 128:144]
        gvar = small[:, 144:160]
        gsd = small[:, 160:176]
        ss = small[:, 0:16]
        sd = small[:, 16:32]
        rstd = small[:, 32:48]

        xn = work[:, 0:2048].rearrange("p (t d) -> p t d", t=TT)
        uT = work[:, 2048:4096].rearrange("p (k t) -> p k t", k=KT)
        hT = work[:, 4096:4096 + FT * T].rearrange("p (f t) -> p f t", f=FT)
        sl = work[:, 10240:10752].rearrange("p (b t) -> p b t", b=2)
        qTr = work[:, 4096:6144].rearrange("p (h x t) -> p h x t", h=RH, x=2)
        kTr = work[:, 6144:8192].rearrange("p (h x t) -> p h x t", h=RH, x=2)
        ogT = work[:, 4096:8192].rearrange("p (k t) -> p k t", k=16)
        vtok = work[:, 8192:12288].rearrange("p (t d) -> p t d", t=TT)
        og = work[:, 12288:16384].rearrange("p (t d) -> p t d", t=TT)
        tab = work[:, 16384:18432]
        ST = work[:, 18432:19968].rearrange("p (h c) -> p h c", h=RH)
        rot = work[:, 0:1024].rearrange("p (y x t) -> p y x t", y=2, x=2)
        osq = work[:, 1024:1536]
        rss = small[:, 48:56]
        rsd = small[:, 56:64]
        rrs = small[:, 176:184]
        xeT = work[:, 4096:6144].rearrange("p (b k s) -> p b k s", b=2, k=KT)
        oh = work[:, 6144:6400].rearrange("p (t s) -> p t s", t=TT)
        ohg = work[:, 6400:6656].rearrange("p (t s) -> p t s", t=TT)
        ohT = work[:, 6656:6912]
        s1 = work[:, 7168:8192].rearrange("p (b f) -> p b f", b=2)
        act = work[:, 8192:9216].rearrange("p (b f) -> p b f", b=2)
        actT = work[:, 9216:10240].rearrange("p (b g s) -> p b g s", b=2, g=4)
        ysb = work[:, 10240:11264]
        gfin = work[:, 11264:12288]
        rw = lambda a, n: route[:, a:a + n]

        s_x = sem("x_loaded")
        s_c = sem("tables_loaded")
        s_q = sem("rwkv_tables_loaded")
        s_tab = sem("retention_tables_loaded")
        s_gf = sem("final_gain_loaded")
        s_ra = [sem(f"rwkv_weights_{i}") for i in range(2)]
        s_w = [sem(f"weights_{i}") for i in range(RING)]
        s_free = sem("weights_used")
        s_ss = sem("squares_summed")
        s_ms = sem("mean_square_ready")
        s_sd = sem("root_ready")
        s_rs = sem("rstd_ready")
        s_xn = sem("normed_ready")
        s_nt = sem("norm_transposed")
        s_uTa = sem("uT_by_scalar")
        s_uTd = sem("uT_by_vector")
        s_h = sem("residual_updated")
        d_step = sem("vector_step")
        a_step = sem("scalar_step")
        p_step = sem("pool_step")
        s_mix = sem("mix_ready")
        s_pj = sem("projection_ready")
        s_pe = sem("projection_stored")
        s_d = sem("decay_ready")
        s_kkr = sem("kk_raw_ready")
        s_sq = sem("kk_squared")
        s_nrm = sem("kk_norm_ready")
        s_pz = sem("pool_zeroed")
        s_g = sem("cumulated_decay_ready")
        s_BK = sem("BK_ready")
        s_AR = sem("AR_ready")
        s_BKh = sem("BKhat_ready")
        s_z = sem("bonus_products_ready")
        s_uv = sem("V_in_place")
        s_cb = sem("gate_terms_ready")
        s_job = sem("core_bank_ready")
        s_jd = sem("core_stored_by_vector")
        s_ja = sem("core_stored_by_scalar")
        s_bd = sem("block_diagonals_ready")
        s_zset = sem("inverse_buffers_zeroed")
        s_T0 = sem("first_merge_ready")
        s_gv = sem("group_variance_ready")
        s_gs = sem("group_root_ready")
        s_yg = sem("gated_y_ready")
        s_ygt = sem("gated_y_transposed")
        s_ygT = sem("ygT_ready")
        s_acc = sem("block_output_ready")
        s_fh = sem("ffn_hidden_ready")
        s_fs = sem("ffn_silu_ready")
        s_fa = sem("ffn_act_ready")
        s_rj = sem("retention_bank_ready")
        s_rd = sem("retention_stored_by_vector")
        s_rA = sem("retention_stored_by_scalar")
        s_oss = sem("o_squares_ready")
        s_om = sem("o_mean_square_ready")
        s_or = sem("o_root_ready")
        s_lg = sem("logits_ready")
        s_ms2 = sem("masks_ready")
        s_cum = sem("positions_ready")
        s_dt = sem("gate_difference_ready")
        s_de = sem("gate_exp_ready")
        s_tabr = sem("routing_ready")
        s_oh = sem("one_hot_ready")
        s_gp = sem("moe_small_bank_ready")
        s_gd = sem("moe_small_stored_by_vector")
        s_ga = sem("moe_small_stored_by_scalar")
        s_mh = sem("moe_hidden_ready")
        s_m1 = sem("moe_silu_ready")
        s_ma = sem("moe_act_ready")
        s_y = sem("expert_output_ready")
        s_ye = sem("expert_output_stored")
        s_fin = sem("final_ready")
        s_out = sem("output_written")

        J_T1, J_G1, J_W, J_A, J_G, J_K, J_R, J_SS, J_V = 0, 1, 2, 6, 10, 14, 18, 22, 26
        def inverse_jobs(c):
            js = [("Q", c, i) for i in range(4)] + [("M", c, i) for i in range(4)]
            for lv in range(1, LEVELS):
                if lv < LEVELS - 1:
                    js += [("W", c, lv), ("WT", c, lv), ("T", c, lv), ("TT", c, lv)]
                else:
                    js += [("WT", c, lv), ("TT", c, lv)]
            return js

        def chain_jobs(c):
            return ([("P", c, 0)] + [("X", c, 0)] * (c > 0) + [("U", c, 0), ("U", c, 1)]
                    + [("S", c, 0)] * (c < NC - 1) + [("Y", c, 0), ("Y", c, 1)])

        def zipped(a, b):
            o = []
            for i in range(max(len(a), len(b))):
                o += a[i:i + 1] + b[i:i + 1]
            return o

        jobs = [("B", i, 0) for i in range(8)] + [("Z", 0, 0)]
        jobs += zipped(inverse_jobs(0), inverse_jobs(1)) + chain_jobs(0)
        jobs += zipped(inverse_jobs(2), chain_jobs(1)) + zipped(inverse_jobs(3), chain_jobs(2)) + chain_jobs(3)
        jobs += [("G", i, 0) for i in range(4)]
        by_act = {"B", "P", "Y", "G"}

        def stored_by(job):
            kind, _, n = job
            return "a" if kind in by_act or (kind == "U" and n == 0) else "d"

        number = {j: n for n, j in enumerate(jobs)}
        count = {}
        for who in "ad":
            seen = 0
            for j in jobs:
                if stored_by(j) == who:
                    seen += 1
                    count[j] = seen

        def stored(job):
            return (s_ja if stored_by(job) == "a" else s_jd), count[job]

        def made(job):
            return s_job, number[job] + 1

        def bd_count(c, lv):
            order = [j for j in jobs if j[0] == "TT" or (j[0], j[2]) == ("M", 3)]
            key = ("M", c, 3) if lv == 0 else ("TT", c, lv)
            return order.index(key) + 1

        first_merges = [j[1] for j in jobs if (j[0], j[2]) == ("M", 3)]

        rjobs = [("q", i, "d") for i in range(RH)] + [("k", i, "d") for i in range(RH)]
        rjobs += [("s", i, "d") for i in range(RH)] + [("v", i, "a") for i in range(8)] + [("g", i, "a") for i in range(8)]
        rjobs += [("o", i, "d") for i in range(8)] + [("t", i, "da"[i % 2]) for i in range(8)]
        rnum = {j[:2]: n for n, j in enumerate(rjobs)}
        rcount = {}
        for who in "ad":
            mine = [j for j in rjobs if j[2] == who]
            rcount.update({j[:2]: n + 1 for n, j in enumerate(mine)})
        rwho = {j[:2]: j[2] for j in rjobs}

        def rstored(job):
            return (s_rA if rwho[job] == "a" else s_rd), rcount[job]

        block = ctx.enter_context(nc.Block())

        @block.sync
        def _(sp):
            sp.dma_start(h[:, :].rearrange("p (t d) -> p t d", t=TT), x).then_inc(s_x, 16)
            used_after = {2: J_A + 4, 3: J_G + 4, 4: J_K + 2, 5: J_K + 4, 6: J_R + 2, 7: J_R + 4, 8: J_V + 2, 9: J_V + 4}
            for i in range(R_SLOTS):
                if i >= 2:
                    sp.wait_ge(s_pj, used_after[i])
                if i == R_SLOTS - 1:
                    sp.wait_ge(s_ygT, 4)
                sp.dma_start(slot(i % 2), rstream[i]).then_inc(s_ra[i % 2], 16)
            for i in (2, 3, 4, 5, 6):
                sp.dma_start(slot(i), pstream[i]).then_inc(s_w[i], 16)
            for i in (0, 1):
                sp.wait_ge(s_acc, 2 + 2 * i)
                sp.dma_start(slot(i), pstream[i]).then_inc(s_w[i], 16)
            for i in range(RING, RING + 5):
                sp.wait_ge(s_free, i - RING + 1)
                sp.dma_start(slot(i % RING), pstream[i]).then_inc(s_w[i % RING], 16)
            with sp.Fori(0, (PRE - RING - 5) // RING) as g:
                for j in range(RING):
                    i = RING + 5 + j
                    sp.wait_ge(s_free, g * RING + (i - RING + 1))
                    sp.dma_start(slot(i % RING), pstream[bass.ds(g * RING + i, 1), :, :].rearrange(
                        "a p n -> p (a n)")).then_inc(s_w[i % RING], 16)
            with sp.Fori(0, NE * E_SLOTS // RING) as g:
                for j in range(RING):
                    i = PRE + j
                    sp.wait_ge(s_free, g * RING + (i - RING + 1))
                    sp.dma_start(slot(i % RING), mstream[bass.ds(g * RING + j, 1), :, :].rearrange(
                        "a p n -> p (a n)")).then_inc(s_w[i % RING], 16)
            sp.wait_ge(s_tabr, 1)
            extras = sp.value_load(itab[0:1, 0:1], min_val=0, max_val=EXTRA)
            for n in range(EXTRA):
                with sp.If(extras > n):
                    e = sp.value_load(itab[0:1, n + 1:n + 2], min_val=0, max_val=NE - 1)
                    base = PRE + (NE + n) * E_SLOTS
                    with sp.Fori(0, E_SLOTS // RING) as g:
                        for j in range(RING):
                            i = base + j
                            sp.wait_ge(s_free, g * RING + (i - RING + 1))
                            sp.dma_start(slot(i % RING), mstream[bass.ds(e * E_SLOTS + g * RING + j, 1), :, :]
                                         .rearrange("a p n -> p (a n)")).then_inc(s_w[i % RING], 16)
                with sp.Else():
                    sp.nop()
            sp.wait_ge(s_fin, TT)
            sp.dma_start(out, xn).then_inc(s_out, 16)
            sp.wait_ge(s_out, 16)

        @block.gpsimd
        def _(pool):
            chain = [0]

            def link(ins):
                chain[0] += 1
                ins.then_inc(p_step, 1)
                pool.wait_ge(p_step, chain[0])

            nc.gpsimd.memset(blk(12, 2), 0.0).then_inc(s_pz, 1)
            pool.wait_ge(s_nt, 4)
            nc.gpsimd.memset(d1T, 0.0).then_inc(s_pz, 1)
            pool.wait_ge(s_pe, J_V + 4)
            pool.wait_ge(s_pz, 2)
            for c in range(NC):
                r0 = 64 * (c % 2)
                nc.gpsimd.tensor_copy(UV[r0:r0 + 64, c], vtok_r[r0:r0 + 64, c // 2, :].rearrange(
                    "p (h v) -> p h v", h=NH)).then_inc(s_uv, 1)
                pool.wait_ge(s_uv, c + 1)
            pool.wait_ge(s_BK, 4)
            pool.wait_ge(s_AR, 3)
            nc.gpsimd.memset(sets[0]["bds"][0], 0.0).then_inc(s_zset, 1)
            nc.gpsimd.memset(sets[0]["bds"][1], 0.0).then_inc(s_zset, 1)
            pool.wait_ge(s_job, 8)
            nc.gpsimd.memset(sets[1]["bds"][0], 0.0).then_inc(s_zset, 1)
            nc.gpsimd.memset(sets[1]["bds"][1], 0.0).then_inc(s_zset, 1)
            pool.wait_ge(s_pj, J_V + 4)
            nc.gpsimd.memset(ring[:, SLOT + 2048:2 * SLOT], 0.0).then_inc(s_zset, 1)
            pool.wait_ge(*stored(("Z", 0, 0)))
            pool.wait_ge(s_uv, NC)
            pool.wait_ge(s_q, 48)
            v4 = vtok_r.rearrange("p t (h v) -> p (t h) v", h=NH)
            link(nc.gpsimd.tensor_tensor(v4, v4, bon.rearrange("p t h -> p (t h)").unsqueeze(2).to_broadcast(
                [P, TT * NH, HN]), ALU.mult))
            link(nc.gpsimd.tensor_tensor(vtok_r, vtok_r, gnb.unsqueeze(1).to_broadcast([P, TT, D]), ALU.add))
            nc.gpsimd.tensor_tensor(vtok_r, vtok_r, gtok, ALU.mult).then_inc(s_cb, 1)
            nc.gpsimd.tensor_tensor(gtok, gtok, gnw.unsqueeze(1).to_broadcast([P, TT, D]), ALU.mult).then_inc(s_cb, 1)

        @block.scalar
        def _(a):
            a.dma_start(cst[:, :], consts).then_inc(s_c, 16)
            a.dma_start(par[:, :], params).then_inc(s_c, 16)
            a.dma_start(qc, qconsts).then_inc(s_q, 16)
            a.dma_start(gnw, rows[0:1, :].to_broadcast([P, D])).then_inc(s_q, 16)
            a.dma_start(gnb, rows[1:2, :].to_broadcast([P, D])).then_inc(s_q, 16)
            act_f = nc.scalar.activation

            def norm_squares(n):
                if n == 0:
                    a.wait_ge(s_x, 16)
                else:
                    a.wait_ge(s_h, 4 * n)
                for t in range(TT):
                    act_f(xn[:, t, :], hv[:, t, :], ACT.Square,
                          accum_out=ss[:, 2 * n + t:2 * n + t + 1]).then_inc(s_ss, 1)
                a.wait_ge(s_ms, n + 1)
                act_f(sd[:, 2 * n:2 * n + 2], rstd[:, 2 * n:2 * n + 2], ACT.Sqrt).then_inc(s_sd, 1)

            def norm_gain(n, v, dst):
                a.wait_ge(s_nt, 4 * (n + 1))
                for k in (0, 1, 4, 5):
                    act_f(dst[:, k, :], ps[:, k // 2, (k % 2) * T:(k % 2 + 1) * T], ACT.Copy, scale=vec(v, k)).then_inc(s_uTa, 1)

            a.wait_ge(s_c, 32)
            norm_squares(0)
            norm_gain(0, V_NM0, uT_r)

            def take(j):
                a.wait_ge(s_pj, j + 1)
                return ps[:, j % 8, :]

            b = take(J_T1)
            act_f(lor[0:64, :], b[0:64, 0:T], ACT.Tanh)
            act_f(lor[64:128, :], b[64:128, 0:T], ACT.Copy).then_inc(s_pe, 1)
            b = take(J_G1)
            act_f(sg1, b[:, 0:T], ACT.Sigmoid)
            act_f(sg2, b[0:32, T:2 * T], ACT.Sigmoid).then_inc(s_pe, 1)
            for base, dst, v in ((J_W, dT, V_W0), (J_A, aT, V_A0)):
                for q in range(4):
                    b = take(base + q)
                    for i in range(2):
                        k = 2 * q + i
                        ins = act_f(fm(dst)[:, k, :], b[:, i * T:(i + 1) * T], ACT.Sigmoid, bias=vec(v, k))
                    ins.then_inc(s_pe, 1)
            a.wait_ge(s_pe, J_A + 4)
            act_f(dT, dT, ACT.Exp, scale=-math.exp(-0.5)).then_inc(s_d, 1)
            for q in range(4):
                b = take(J_G + q)
                act_f(gtok[:, q % 2, (q // 2) * 512:(q // 2 + 1) * 512], b, ACT.Copy).then_inc(s_pe, 1)
            for base, dst in ((J_K, kT), (J_R, rT)):
                for q in range(4):
                    b = take(base + q)
                    act_f(dst[:, q * 512:(q + 1) * 512], b, ACT.Copy).then_inc(s_pe, 1)
                if base == J_K:
                    a.wait_ge(s_kkr, 1)
                    a.wait_ge(s_g, 1)
                    act_f(sqT, kkT, ACT.Square).then_inc(s_sq, 1)
            for q in range(4):
                b = take(J_SS + q)
                act_f(sqT[:, q * 512:(q + 1) * 512], b, ACT.Sqrt).then_inc(s_pe, 1)
            for q in range(4):
                b = take(J_V + q)
                act_f(vtok_r[:, q % 2, (q // 2) * 512:(q // 2 + 1) * 512], b, ACT.Copy).then_inc(s_pe, 1)

            for j in jobs:
                kind, c, n = j
                bank = ps[:, number[j] % 8, :]
                up = 64 * (1 - c % 2)
                if stored_by(j) == "a":
                    a.wait_ge(*made(j))
                    if kind == "B":
                        act_f(BKT[:, c].rearrange("p c k -> p (c k)"), bank, ACT.Copy).then_inc(s_ja, 1)
                    elif kind == "P":
                        if c >= 1:
                            a.wait_ge(*made(("U", c - 1, 1)))
                        act_f(Xst.rearrange("p n v -> p (n v)"), bank, ACT.Copy).then_inc(s_ja, 1)
                    elif kind == "U":
                        act_f(UV[up:up + 64, c, 0:8, :].rearrange("p h v -> p (h v)"), bank[up:up + 64, :],
                              ACT.Copy).then_inc(s_ja, 1)
                    elif kind == "Y":
                        r0 = 64 * (c % 2)
                        act_f(yS[r0:r0 + 64, c // 2, 8 * n:8 * n + 8, :].rearrange("p h v -> p (h v)"),
                              bank[r0:r0 + 64, :], ACT.Copy).then_inc(s_ja, 1)
                        if n == 1 and c % 2:
                            a.wait_ge(s_gv, c // 2 + 1)
                            act_f(gsd, gvar, ACT.Sqrt).then_inc(s_gs, 1)
                    elif kind == "G":
                        t, half = c // 2, c % 2
                        act_f(ygT[:, 4 * half:4 * half + 4, t * P:(t + 1) * P],
                              bank.rearrange("p (k s) -> p k s", k=4), ACT.Copy).then_inc(s_ygT, 1)
                if (kind == "M" and n == 3) or (kind == "TT" and n < LEVELS):
                    s = sets[c % 2]
                    lv = 0 if kind == "M" else n
                    a.wait_ge(*made(j))
                    if lv == 0:
                        a.wait_ge(s_T0, first_merges.index(c) + 1)
                        a.wait_ge(s_zset, 2 + 2 * (c % 2))
                    else:
                        a.wait_ge(*stored(j))
                    for src, dst in (("T", "bdT"), ("TT", "bdTT")):
                        if lv == LEVELS - 1 and src == "T":
                            continue
                        for i in range(2):
                            r = slice(64 * i, 64 * i + 64)
                            ins = act_f(s[dst][r, :, r], s[src][r], ACT.Copy)
                    ins.then_inc(s_bd, 1)

            norm_squares(1)
            norm_gain(1, V_NF0, uT)
            for f in range(FT):
                a.wait_ge(s_fh, f + 1)
                if f >= 2:
                    a.wait_ge(s_fa, f - 1)
                act_f(sl[:, f % 2, :], ps[:, f % 4, 0:T], ACT.Silu).then_inc(s_fs, 1)

            norm_squares(2)
            a.dma_start(tab, tabs).then_inc(s_tab, 16)
            norm_gain(2, V_NM1, uT)
            for j in rjobs:
                kind, i, who = j
                bank = ps[:, rnum[j[:2]] % 8, :]
                if kind == "o":
                    a.wait_ge(s_rj, rnum[j[:2]] + 1)
                    if i >= 1:
                        a.wait_ge(s_oss, i)
                    act_f(osq, bank, ACT.Square, accum_out=rss[:, i:i + 1]).then_inc(s_oss, 1)
                    if i == 7:
                        a.wait_ge(s_om, 1)
                        act_f(rsd, rss, ACT.Sqrt).then_inc(s_or, 1)
                if who != "a":
                    continue
                a.wait_ge(s_rj, rnum[j[:2]] + 1)
                if kind in "vg":
                    dst = vtok if kind == "v" else og
                    act_f(dst[:, i % 2, (i // 2) * 512:(i // 2 + 1) * 512], bank,
                          ACT.Copy if kind == "v" else ACT.Silu).then_inc(s_rA, 1)
                else:
                    t, kg = i // 4, i % 4
                    act_f(ogT[:, 4 * kg:4 * kg + 4, t * P:(t + 1) * P], bank.rearrange("p (k s) -> p k s", k=4),
                          ACT.Copy).then_inc(s_rA, 1)

            norm_squares(3)
            a.dma_start(gfin, rows[2:3, :].to_broadcast([P, D])).then_inc(s_gf, 16)
            norm_gain(3, V_NF1, uT)
            a.wait_ge(s_dt, 1)
            act_f(rw(48, 2), rw(44, 2), ACT.Exp).then_inc(s_de, 1)
            a.wait_ge(s_tabr, 1)
            extras = a.value_load(itab[0:1, 0:1], min_val=0, max_val=EXTRA)
            with a.Fori(0, extras + NE) as e:
                for g in range(2):
                    a.wait_ge(s_gp, e * 14 + (g + 1))
                    for q in range(4):
                        k = 4 * g + q
                        ins = act_f(xeT[:, 0, k, :], ps[:, 7 - g, q * P:(q + 1) * P], ACT.Copy, scale=vec(V_NF1, k))
                    ins.then_inc(s_ga, 1)
                for j in range(FJ + 1):
                    if j < FJ:
                        a.wait_ge(s_mh, e * FJ + (j + 1))
                        if j >= 2:
                            a.wait_ge(s_ma, e * FJ + (j - 1))
                        act_f(s1[:, j % 2, :], ps[:, 2 * (j % 2), :], ACT.Silu).then_inc(s_m1, 1)
                    if j >= 1:
                        i = j - 1
                        a.wait_ge(s_gp, e * 14 + (4 + i))
                        act_f(actT[:, i % 2], ps[:, 7 - (3 + i) % 2, :].rearrange("p (g s) -> p g s", g=4),
                              ACT.Copy).then_inc(s_ga, 1)
            a.wait_ge(s_gd, (extras + NE) * 5)
            for t in range(TT):
                n = 4
                act_f(uT.rearrange("p k t -> p (k t)")[:, t * D:(t + 1) * D], hv[:, t, :], ACT.Square,
                      accum_out=ss[:, 2 * n + t:2 * n + t + 1]).then_inc(s_ss, 1)
            a.wait_ge(s_ms, 5)
            act_f(sd[:, 8:10], rstd[:, 8:10], ACT.Sqrt).then_inc(s_sd, 1)

        @block.vector
        def _(v):
            chain = [0]
            V = nc.vector

            def link(ins):
                chain[0] += 1
                ins.then_inc(d_step, 1)
                v.wait_ge(d_step, chain[0])

            def rsqrt(m, r, t):
                link(V.reciprocal(r, r))
                link(V.tensor_tensor(t, r, r, ALU.mult))
                link(V.tensor_tensor(t, t, m, ALU.mult))
                link(V.tensor_scalar(t, t, -0.5, 1.5, ALU.mult, ALU.add))
                link(V.tensor_tensor(r, r, t, ALU.mult))

            def norm_scale(n, dst):
                m = rstd[:, 2 * n:2 * n + 2]
                r = sd[:, 2 * n:2 * n + 2]
                v.wait_ge(s_ss, 2 * n + 2)
                V.tensor_scalar(m, ss[:, 2 * n:2 * n + 2], 1.0 / D, EPS, ALU.mult, ALU.add).then_inc(s_ms, 1)
                v.wait_ge(s_sd, n + 1)
                rsqrt(m, r, small[:, 184:186])
                for t in range(TT):
                    V.tensor_scalar(dst[:, t, :], hv[:, t, :], r[:, t:t + 1], None, ALU.mult).then_inc(s_xn, 1)

            def norm_gain(n, vn, dst):
                v.wait_ge(s_nt, 4 * (n + 1))
                for k in (2, 3, 6, 7):
                    V.tensor_scalar(dst[:, k, :], ps[:, k // 2, (k % 2) * T:(k % 2 + 1) * T], vec(vn, k), None,
                                    ALU.mult).then_inc(s_uTd, 1)

            def add_to_h(n):
                for q in range(4):
                    v.wait_ge(s_acc, 4 * n + q + 1)
                    c, t = q // 2, q % 2
                    dst = hv[:, t, c * 512:(c + 1) * 512]
                    V.tensor_tensor(dst, dst, ps[:, 4 + q, :], ALU.add).then_inc(s_h, 1)
                v.wait_ge(s_h, 4 * n + 4)

            v.wait_ge(s_c, 32)
            v.wait_ge(s_x, 16)
            norm_scale(0, xn)
            norm_gain(0, V_NM0, uT_r)
            v.wait_ge(s_uTd, 4)
            v.wait_ge(s_uTa, 4)
            link(V.tensor_tensor(dxT[:, :, 1:T], uT_r[:, :, 0:T - 1], uT_r[:, :, 1:T], ALU.subtract))
            link(V.tensor_scalar(dxT[:, :, 0:1], uT_r[:, :, 0:1], -1.0, None, ALU.mult))
            for m, row in enumerate((1, 4, 5, 2, 0, 3)):
                if m >= 2:
                    v.wait_ge(s_pj, (1, 1, 2, J_K + 4)[m - 2])
                for k in range(KT):
                    ins = V.scalar_tensor_tensor(out=mix[m % 2][:, k, :], in0=dxT[:, k, :], scalar=vec(V_MU + row, k),
                                                 in1=uT_r[:, k, :], op0=ALU.mult, op1=ALU.add)
                ins.then_inc(s_mix, 1)
                if m == 3:
                    v.wait_ge(s_d, 1)
                    v.wait_ge(s_pz, 2)
                    d0 = dT.rearrange("p (c t) -> p c t", t=CH)[:, :, 0:1]
                    link(V.tensor_copy(d1T.rearrange("p (c t) -> p c t", t=CH)[:, :, 0:1], d0))
                    link(V.memset(d0, 0.0))
                    V.tensor_tensor_scan(gT, dT, d1T, 0.0, ALU.mult, ALU.add).then_inc(s_g, 1)
                    v.wait_ge(s_g, 1)
                    V.reciprocal(giT, gT)
                    V.tensor_copy(gC.unsqueeze(2), gT.rearrange("p (c t) -> p c t", t=CH)[:, :, CH - 1:CH])
                    for k in range(KT):
                        ins = V.tensor_scalar(fm(kmT)[:, k, :], fm(aT)[:, k, :], 1.0, vec(V_KA, k),
                                              ALU.subtract, ALU.mult)
                    link(ins)
            v.wait_ge(s_pe, J_K + 4)
            for k in range(KT):
                ins = V.tensor_scalar(fm(kkT)[:, k, :], fm(kT)[:, k, :], vec(V_KK, k), None, ALU.mult)
            ins.then_inc(s_kkr, 1)
            V.scalar_tensor_tensor(out=kmT, in0=kmT, scalar=1.0, in1=kT, op0=ALU.add, op1=ALU.mult).then_inc(s_kkr, 1)
            v.wait_ge(s_pe, J_SS + 4)
            link(V.tensor_scalar(sqT, sqT, 1e-12, None, ALU.max))
            link(V.reciprocal(sqT, sqT))
            link(V.tensor_tensor(kkT, kkT, sqT, ALU.mult))
            link(V.tensor_tensor(aT, kkT, aT, ALU.mult))
            c4 = lambda z: z.rearrange("p (n c t) -> p n c t", n=NP, c=NC)
            v.wait_ge(s_mix, 6)
            for o in range(2):
                for pos, src in ((o, kmT), (1 - o, aT)):
                    V.tensor_tensor(BK[:, :, o::2, pos, :], c4(src)[:, :, o::2, :], c4(giT)[:, :, o::2, :],
                                    ALU.mult).then_inc(s_BK, 1)
            c3 = lambda z: z.rearrange("p (c t) -> p c t", t=CH)
            A3 = AR.rearrange("p n c x t -> p (n c) x t")
            V.scalar_tensor_tensor(out=A3[:, :, 0, 1:CH], in0=c3(kkT)[:, :, 1:CH], scalar=-1.0,
                                   in1=c3(gT)[:, :, 0:CH - 1], op0=ALU.mult, op1=ALU.mult).then_inc(s_AR, 1)
            V.tensor_scalar(A3[:, :, 0, 0:1], c3(kkT)[:, :, 0:1], -1.0, None, ALU.mult).then_inc(s_AR, 1)
            V.tensor_tensor(A3[:, :, 1, :], c3(rT), c3(gT), ALU.mult).then_inc(s_AR, 1)
            v.wait_ge(s_AR, 3)
            for k in range(KT):
                ins = V.scalar_tensor_tensor(out=fm(rT)[:, k, :], in0=fm(rT)[:, k, :], scalar=vec(V_RK, k),
                                             in1=fm(kmT)[:, k, :], op0=ALU.mult, op1=ALU.mult)
            ins.then_inc(s_z, 1)
            v.wait_ge(s_BK, 4)
            V.tensor_tensor(BKh.rearrange("p n c k -> p (n c) k"), BK.rearrange("p n c x t -> p (n c) (x t)"),
                            gC.unsqueeze(2).to_broadcast([P, 32, P]), ALU.mult).then_inc(s_BKh, 1)

            v.wait_ge(s_q, 48)
            lev = lambda n, up: qc[:, Q_LEV + 128 * n + 64 * up:Q_LEV + 128 * n + 64 * up + 64]
            for j in jobs:
                kind, c, n = j
                bank = ps[:, number[j] % 8, :]
                s = sets[c % 2]
                b3 = bank.rearrange("p (n s) -> p n s", n=NP)
                if stored_by(j) == "d":
                    v.wait_ge(*made(j))
                if kind == "Z":
                    V.tensor_copy(bon.rearrange("p t h -> p (t h)"), bank[:, 0:32]).then_inc(s_jd, 1)
                elif kind == "Q":
                    par_, half = n // 2, n % 2
                    if n == 0 and c >= 2:
                        v.wait_ge(*made(("Y", c - 2, 1)))
                    V.tensor_tensor(Qm[c % 2][:, 8 * half + par_:8 * half + 8:2, :],
                                    bank.rearrange("p (h t) -> p h t", h=4),
                                    qc[:, Q_MASK:Q_MASK + P].unsqueeze(1).to_broadcast([P, 4, P]),
                                    ALU.mult).then_inc(s_jd, 1)
                elif kind == "M":
                    i, up = n % 2, n // 2
                    r = slice(64 * i, 64 * i + 64)
                    if n == 0:
                        v.wait_ge(s_zset, 2 + 2 * (c % 2))
                        if c >= 2:
                            v.wait_ge(*made(("U", c - 2, 1)))
                    mk = qc[r, (Q_MU if up else Q_ML):(Q_MU if up else Q_ML) + 64]
                    V.tensor_tensor(s["bdMT" if up else "bdM"][r, :, r], b3[r],
                                    mk.unsqueeze(1).to_broadcast([64, NP, 64]), ALU.mult).then_inc(s_jd, 1)
                    if n == 3:
                        v.wait_ge(s_jd, count[j])
                        eye = qc[:, Q_EYE:Q_EYE + 64]
                        for src, dst, up in (("bdM", "T", 0), ("bdMT", "TT", 1)):
                            for i in range(2):
                                r = slice(64 * i, 64 * i + 64)
                                ins = V.tensor_tensor(s[dst][r], s[src][r, :, r],
                                                      lev(0, up)[r].unsqueeze(1).to_broadcast([64, NP, 64]), ALU.mult)
                        link(ins)
                        for dst in ("T", "TT"):
                            ins = V.tensor_tensor(s[dst], s[dst], eye.unsqueeze(1).to_broadcast([P, NP, 64]), ALU.add)
                        ins.then_inc(s_T0, 1)
                elif kind in ("W", "WT"):
                    V.tensor_tensor(s[kind], b3, lev(n, int(kind == "WT")).unsqueeze(1).to_broadcast([P, NP, 64]),
                                    ALU.mult).then_inc(s_jd, 1)
                elif kind in ("T", "TT"):
                    if kind == "T" and n == 1:
                        v.wait_ge(s_T0, first_merges.index(c) + 1)
                    v.wait_ge(s_bd, bd_count(c, n - 1))
                    V.tensor_tensor(s[kind], s[kind], b3, ALU.add).then_inc(s_jd, 1)
                elif kind == "X":
                    v.wait_ge(*stored(("P", c, 0)))
                    V.tensor_tensor(Xst, Xst, b3, ALU.add).then_inc(s_jd, 1)
                elif kind == "U" and n == 1:
                    up = 64 * (1 - c % 2)
                    V.tensor_copy(UV[up:up + 64, c, 8:16, :].rearrange("p h v -> p (h v)"),
                                  bank[up:up + 64, :]).then_inc(s_jd, 1)
                elif kind == "S":
                    new, old = bdS[(c + 1) % 2], bdS[c % 2]
                    if c == 0:
                        v.wait_ge(s_zset, 5)
                    else:
                        v.wait_ge(*made(("Y", c - 1, 1)))
                    for i in range(2):
                        r = slice(64 * i, 64 * i + 64)
                        if c == 0:
                            ins = V.tensor_copy(new[r, :, r], b3[r])
                        else:
                            g = gC.rearrange("p (n c) -> p n c", c=NC)[r, :, c:c + 1].to_broadcast([64, NP, 64])
                            link(V.tensor_tensor(new[r, :, r], old[r, :, r], g, ALU.mult))
                            ins = V.tensor_tensor(new[r, :, r], new[r, :, r], b3[r], ALU.add)
                    ins.then_inc(s_jd, 1)
                if kind == "Y" and n == 1 and c % 2:
                    t = c // 2
                    y = yS[:, t]
                    tmp = UV[:, 0]
                    bc = lambda z: z.unsqueeze(2).to_broadcast([P, NH, HN])
                    v.wait_ge(*stored(j))
                    link(V.tensor_reduce(gsum, y, AX.X, ALU.add))
                    link(V.tensor_scalar(gsum, gsum, 1.0 / HN, None, ALU.mult))
                    link(V.tensor_tensor(y, y, bc(gsum), ALU.subtract))
                    link(V.tensor_tensor(tmp, y, y, ALU.mult))
                    link(V.tensor_reduce(gvar, tmp, AX.X, ALU.add))
                    V.tensor_scalar(gvar, gvar, 1.0 / HN, GN_EPS, ALU.mult, ALU.add).then_inc(s_gv, 1)
                    v.wait_ge(s_gs, t + 1)
                    rsqrt(gvar, gsd, gsum)
                    link(V.tensor_tensor(y, y, bc(gsd), ALU.mult))
                    v.wait_ge(s_cb, 2)
                    yf = y.rearrange("p h v -> p (h v)")
                    link(V.tensor_tensor(yf, yf, gtok[:, t, :], ALU.mult))
                    V.tensor_tensor(yf, yf, vtok_r[:, t, :], ALU.add).then_inc(s_yg, 1)
            add_to_h(0)

            norm_scale(1, xn)
            norm_gain(1, V_NF0, uT)
            for f in range(FT):
                v.wait_ge(s_fs, f + 1)
                V.tensor_tensor(hT[:, f, :], sl[:, f % 2, :], ps[:, f % 4, T:2 * T], ALU.mult).then_inc(s_fa, 1)
            add_to_h(1)

            norm_scale(2, xn)
            norm_gain(2, V_NM1, uT)
            v.wait_ge(s_tab, 16)
            both = lambda a: tab[:, a:a + T].unsqueeze(1).to_broadcast([P, 2, T])
            for j in rjobs:
                kind, i, who = j
                bank = ps[:, rnum[j[:2]] % 8, :]
                if who != "d":
                    continue
                v.wait_ge(s_rj, rnum[j[:2]] + 1)
                if kind in "qk":
                    dst = qTr if kind == "q" else kTr
                    b2 = bank.rearrange("p (x t) -> p x t", x=2)
                    if rcount[j[:2]] > 1:
                        v.wait_ge(s_rd, rcount[j[:2]] - 1)
                    V.tensor_tensor(rot[:, 0], b2, both(0), ALU.mult)
                    link(V.tensor_tensor(rot[:, 1], b2, both(T), ALU.mult))
                    V.tensor_tensor(dst[:, i, 0, :], rot[:, 0, 0, :], rot[:, 1, 1, :], ALU.subtract)
                    V.tensor_tensor(dst[:, i, 1, :], rot[:, 0, 1, :], rot[:, 1, 0, :], ALU.add).then_inc(s_rd, 1)
                elif kind == "s":
                    V.tensor_tensor(ST[:, i, :], bank[:, 0:384], tab[:, 2 * T + 384 * i:2 * T + 384 * (i + 1)],
                                    ALU.mult).then_inc(s_rd, 1)
                elif kind == "o":
                    hd, t = i // 2, i % 2
                    if i == 0:
                        v.wait_ge(s_oss, 8)
                        V.tensor_scalar(rss, rss, 1.0 / RV, EPS, ALU.mult, ALU.add).then_inc(s_om, 1)
                        v.wait_ge(s_om, 1)
                        v.wait_ge(s_or, 1)
                        rsqrt(rss, rsd, rrs)
                        v.wait_ge(*rstored(("g", 7)))
                    dst = og[:, t, hd * RV:(hd + 1) * RV]
                    V.scalar_tensor_tensor(out=dst, in0=bank, scalar=rsd[:, i:i + 1], in1=dst, op0=ALU.mult,
                                           op1=ALU.mult).then_inc(s_rd, 1)
                else:
                    t, kg = i // 4, i % 4
                    V.tensor_copy(ogT[:, 4 * kg:4 * kg + 4, t * P:(t + 1) * P],
                                  bank.rearrange("p (k s) -> p k s", k=4)).then_inc(s_rd, 1)
            add_to_h(2)

            norm_scale(3, xn)
            norm_gain(3, V_NF1, uT)
            v.wait_ge(s_lg, 1)
            lg = rw(0, 16).rearrange("p (t e) -> p t e", t=TT)
            link(V.tensor_copy(rw(0, 16), ps[:, 7, 0:16]))
            big = rw(64, 128).rearrange("p (x f) -> p x f", f=NE)
            big4 = rw(64, 128).rearrange("p (t e f) -> p t e f", t=TT, e=NE)
            eq = rw(192, 128).rearrange("p (t e f) -> p t e f", t=TT, e=NE)
            rank = rw(16, 16)
            tie = cst[:, C_TIE:C_TIE + 64].rearrange("p (e f) -> p e f", e=NE)
            for t in range(TT):
                mine = lg[:, t, :].unsqueeze(2).to_broadcast([P, NE, NE])
                other = lg[:, t, :].unsqueeze(1).to_broadcast([P, NE, NE])
                V.tensor_tensor(big4[:, t], other, mine, ALU.is_gt)
                link(V.tensor_tensor(eq[:, t], other, mine, ALU.is_equal))
                link(V.tensor_tensor(eq[:, t], eq[:, t], tie, ALU.mult))
            link(V.tensor_tensor(rw(64, 128), rw(64, 128), rw(192, 128), ALU.add))
            link(V.tensor_reduce(rank, big, AX.X, ALU.add))
            is0, is1 = rw(64, 16), rw(80, 16)
            V.tensor_scalar(is0, rank, 0.0, None, ALU.is_equal)
            link(V.tensor_scalar(is1, rank, 1.0, None, ALU.is_equal))
            mask = rw(96, 16)
            V.tensor_tensor(mask, is0, is1, ALU.add).then_inc(s_ms2, 1)
            lgf = rw(0, 16)
            pick = rw(112, 32)
            V.tensor_tensor(rw(112, 16), lgf, is0, ALU.mult)
            link(V.tensor_tensor(rw(128, 16), lgf, is1, ALU.mult))
            link(V.tensor_reduce(rw(40, 4), pick.rearrange("p (x e) -> p x e", e=NE), AX.X, ALU.add))
            V.tensor_tensor(rw(44, 2), rw(42, 2), rw(40, 2), ALU.subtract).then_inc(s_dt, 1)
            v.wait_ge(s_de, 1)
            link(V.tensor_scalar(rw(50, 2), rw(48, 2), 1.0, None, ALU.add))
            link(V.reciprocal(rw(50, 2), rw(50, 2)))
            link(V.tensor_tensor(rw(52, 2), rw(48, 2), rw(50, 2), ALU.mult))
            for t in range(TT):
                V.tensor_scalar(rw(64 + 8 * t, 8), rw(64 + 8 * t, 8), rw(50 + t, 1), None, ALU.mult)
                ins = V.tensor_scalar(rw(80 + 8 * t, 8), rw(80 + 8 * t, 8), rw(52 + t, 1), None, ALU.mult)
            link(ins)
            NI = NE + EXTRA
            keys = rw(192, TT * NI).rearrange("p (t i) -> p t i", t=TT)
            gates = rw(224, TT * NI).rearrange("p (t i) -> p t i", t=TT)
            m3 = mask.rearrange("p (t e) -> p t e", t=TT)
            V.tensor_tensor(gates[:, :, 0:NE], is0.rearrange("p (t e) -> p t e", t=TT),
                            is1.rearrange("p (t e) -> p t e", t=TT), ALU.add)
            v.wait_ge(s_cum, 1)
            V.tensor_tensor(keys[:, :, 0:NE], m3, ps[:, 7, 32:48].rearrange("p (t e) -> p t e", t=TT), ALU.mult)
            over, order = rw(256, NE), rw(264, NE)
            link(V.tensor_scalar(over, ps[:, 7, 48:56], float(P), None, ALU.is_gt))
            link(V.tensor_tensor_scan(order, ones[:, 0:NE], over, 0.0, ALU.mult, ALU.add))
            selx = rw(272, EXTRA * NE).rearrange("p (n e) -> p n e", n=EXTRA)
            for n in range(EXTRA):
                link(V.tensor_scalar(selx[:, n, :], order, float(n + 1), None, ALU.is_equal))
                link(V.tensor_tensor(selx[:, n, :], selx[:, n, :], over, ALU.mult))
            tmp = rw(112, TT * EXTRA * NE)
            tmp4 = tmp.rearrange("p (t n e) -> p t n e", t=TT, n=EXTRA)
            for src, dst in ((keys, keys), (gates, gates)):
                for t in range(TT):
                    for n in range(EXTRA):
                        ins = V.tensor_tensor(tmp4[:, t, n, :], src[:, t, 0:NE], selx[:, n, :], ALU.mult)
                link(ins)
                link(V.tensor_reduce(dst[:, :, NE:NI], tmp4, AX.X, ALU.add))
            link(V.tensor_scalar(keys[:, :, NE:NI], keys[:, :, NE:NI], float(P), None, ALU.subtract))
            tab4 = rw(304, 4)
            V.tensor_copy(tab4[:, 0:1], order[:, NE - 1:NE])
            for n in range(EXTRA):
                ins = V.tensor_tensor(tmp4[:, 0, n, :], cst[:, C_EIDX:C_EIDX + NE], selx[:, n, :], ALU.mult)
            link(ins)
            link(V.tensor_reduce(tab4[:, 1:4], tmp4[:, 0], AX.X, ALU.add))
            V.tensor_copy(itab[:, 0:4], tab4).then_inc(s_tabr, 1)
            v.wait_ge(s_tabr, 1)
            extras = v.value_load(itab[0:1, 0:1], min_val=0, max_val=EXTRA)

            with v.Fori(0, extras + NE) as e:
                for t in range(TT):
                    key = route[:, bass.ds(e + (192 + NI * t), 1)]
                    gate = route[:, bass.ds(e + (224 + NI * t), 1)]
                    V.tensor_copy(small[:, 192 + t:193 + t], key)
                    ins = V.tensor_copy(small[:, 194 + t:195 + t], gate)
                ins.then_inc(s_oh, 1)
                v.wait_ge(s_oh, e * 2 + 1)
                for t in range(TT):
                    V.tensor_scalar(oh[:, t, :], cst[:, C_IOTA:C_IOTA + P], small[:, 192 + t:193 + t], None,
                                    ALU.is_equal)
                    ins = V.tensor_scalar(ohg[:, t, :], cst[:, C_IOTA:C_IOTA + P], small[:, 192 + t:193 + t],
                                          small[:, 194 + t:195 + t], ALU.is_equal, ALU.mult)
                ins.then_inc(s_oh, 1)
                v.wait_ge(s_gp, e * 14 + 3)
                V.tensor_copy(ohT, ps[:, 7, 0:T]).then_inc(s_gd, 1)
                for j in range(FJ):
                    v.wait_ge(s_m1, e * FJ + (j + 1))
                    if j >= 2:
                        v.wait_ge(s_gp, e * 14 + (2 + j))
                    V.tensor_tensor(act[:, j % 2, :], s1[:, j % 2, :], ps[:, 2 * (j % 2) + 1, :],
                                    ALU.mult).then_inc(s_ma, 1)
                v.wait_ge(s_y, e + 1)
                V.tensor_copy(ysb[:, 0:512], ps[:, 4, :])
                V.tensor_copy(ysb[:, 512:1024], ps[:, 5, :]).then_inc(s_ye, 1)
                for q in range(4):
                    v.wait_ge(s_gp, e * 14 + (11 + q))
                    t, c = q // 2, q % 2
                    dst = hv[:, t, c * 512:(c + 1) * 512]
                    V.tensor_tensor(dst, dst, ps[:, 7 - q % 2, :], ALU.add).then_inc(s_gd, 1)
                v.wait_ge(s_gd, e * 5 + 5)
            norm_scale(4, xn)
            v.wait_ge(s_xn, 10)
            v.wait_ge(s_gf, 16)
            for t in range(TT):
                V.tensor_tensor(xn[:, t, :], xn[:, t, :], gfin, ALU.mult).then_inc(s_fin, 1)

        @block.tensor
        def _(pe):
            owed = []

            def M(*args, **kw):
                ins = nc.tensor.matmul(*args, **kw)
                if owed:
                    ins.then_inc(owed.pop(), 1)
                return ins

            def transposes(n):
                pe.wait_ge(s_xn, 2 * n + 2)
                for q in range(4):
                    for k in (2 * q, 2 * q + 1):
                        for t in range(TT):
                            ins = nc.tensor.transpose(ps[:, q, (k % 2) * T + t * P:(k % 2) * T + (t + 1) * P],
                                                      xn[:, t, k * P:(k + 1) * P], ident)
                            if owed:
                                ins.then_inc(owed.pop(), 1)
                    ins.then_inc(s_nt, 1)

            def u_ready(n):
                pe.wait_ge(s_uTa, 4 * n + 4)
                pe.wait_ge(s_uTd, 4 * n + 4)

            pe.wait_ge(s_c, 32)
            transposes(0)

            def job(j):
                if j >= 8:
                    pe.wait_ge(s_pe, j - 7)
                return ps[:, j % 8, :]

            def arrived(i):
                pe.wait_ge(s_ra[i % 2], 16 * (i // 2 + 1))
                return slot(i % 2)

            u_ready(0)
            wa = arrived(0)
            l1 = wa[:, 0:KT * 288].rearrange("p (k n) -> p k n", k=KT)
            l2 = wa[:, KT * 288:KT * 288 + D]
            b = job(J_T1)
            for m in range(2):
                pe.wait_ge(s_mix, m + 1)
                for k in range(KT):
                    ins = M(b[64 * m:64 * m + 64, 0:T], l1[:, k, 64 * m:64 * m + 64], mix[m][:, k, :],
                            start=(k == 0), stop=(k == KT - 1))
            ins.then_inc(s_pj, 1)
            b = job(J_G1)
            pe.wait_ge(s_mix, 3)
            for lo, n, dst in ((128, 128, b[:, 0:T]), (256, 32, b[0:32, T:2 * T])):
                for k in range(KT):
                    ins = M(dst, l1[:, k, lo:lo + n], mix[0][:, k, :], start=(k == 0), stop=(k == KT - 1))
            ins.then_inc(s_pj, 1)
            pe.wait_ge(s_pe, 1)
            for base, r in ((J_W, slice(0, 64)), (J_A, slice(64, 128))):
                for q in range(4):
                    b = job(base + q)
                    for k in (2 * q, 2 * q + 1):
                        ins = M(b[:, (k % 2) * T:(k % 2 + 1) * T], l2[r, k * P:(k + 1) * P], lor[r, :],
                                start=True, stop=True)
                    ins.then_inc(s_pj, 1)
            wb = arrived(1)
            pe.wait_ge(s_pe, 2)
            for q in range(4):
                b, t, n = job(J_G + q), q % 2, q // 2
                M(b, sg1[:, t * P:(t + 1) * P], wb[:, n * 512:(n + 1) * 512], start=True, stop=False)
                M(b, sg2[:, t * P:(t + 1) * P], wb[0:32, D + n * 512:D + (n + 1) * 512], start=False,
                  stop=True).then_inc(s_pj, 1)
            for base, m, i0 in ((J_K, 3, 2), (J_R, 4, 4)):
                pe.wait_ge(s_mix, m + 1)
                for q in range(4):
                    b = job(base + q)
                    w = arrived(i0 + q // 2).rearrange("p (k n) -> p k n", k=KT)
                    for i in range(2):
                        f = 2 * (q % 2) + i
                        for k in range(KT):
                            ins = M(b[:, i * T:(i + 1) * T], w[:, k, f * P:(f + 1) * P], mix[m % 2][:, k, :],
                                    start=(k == 0), stop=(k == KT - 1))
                    ins.then_inc(s_pj, 1)
            pe.wait_ge(s_sq, 1)
            pe.wait_ge(s_q, 48)
            for q in range(4):
                M(job(J_SS + q), qc[:, Q_BO:Q_BO + P], sqT[:, q * 512:(q + 1) * 512], start=True,
                  stop=True).then_inc(s_pj, 1)
            pe.wait_ge(s_mix, 6)
            for q in range(4):
                b, t, n = job(J_V + q), q % 2, q // 2
                w = arrived(6 + n).rearrange("p (k n) -> p k n", k=KT)
                for k in range(KT):
                    ins = M(b, mix[1][:, k, t * P:(t + 1) * P], w[:, k, :], start=(k == 0), stop=(k == KT - 1))
                ins.then_inc(s_pj, 1)

            pe.wait_ge(s_pe, J_V + 4)
            pe.wait_ge(s_uv, NC)
            for j in jobs:
                kind, c, n = j
                i = number[j]
                bank = ps[:, i % 8, :]
                s = sets[c % 2]
                if i >= 8:
                    if jobs[i - 8][0] == "G":
                        pe.wait_ge(s_ygT, jobs[i - 8][1] + 1)
                    else:
                        pe.wait_ge(*stored(jobs[i - 8]))
                if kind == "B":
                    if c == 0:
                        pe.wait_ge(s_BKh, 1)
                    for x_ in range(NC):
                        ins = nc.tensor.transpose(bank[:, x_ * P:(x_ + 1) * P], BKh[:, c, x_, :], ident)
                elif kind == "Z":
                    pe.wait_ge(s_z, 1)
                    for t in range(TT):
                        for p_ in range(NP):
                            ins = M(bank[:, 16 * t + 2 * p_:16 * t + 2 * p_ + 2], fm(rT)[:, p_, t * P:(t + 1) * P],
                                    qc[:, Q_SEL:Q_SEL + 2], start=True, stop=True)
                elif kind == "Q":
                    r = slice(64 * (n // 2), 64 * (n // 2) + 64)
                    for q in range(4):
                        p_ = 4 * (n % 2) + q
                        ins = M(bank[:, q * P:(q + 1) * P], BK[r, p_, c].rearrange("p x t -> p (x t)"),
                                AR[r, p_, c].rearrange("p x t -> p (x t)"), start=True, stop=True)
                elif kind == "M":
                    r = slice(64 * (n % 2), 64 * (n % 2) + 64)
                    for p_ in range(NP):
                        A_, B_ = AR[r, p_, c, 0, :], BK[r, p_, c, 1 - c % 2, :]
                        ins = M(bank[r, p_ * 64:(p_ + 1) * 64], *((A_, B_) if n < 2 else (B_, A_)),
                                start=True, stop=True)
                elif kind in ("W", "WT", "T", "TT"):
                    lhs = {"W": "bdMT", "WT": "bdM", "T": "bdTT", "TT": "bdT"}[kind]
                    rhs = {"W": "T", "WT": "TT", "T": "W", "TT": "WT"}[kind]
                    if kind in ("W", "WT"):
                        if n == 1:
                            pe.wait_ge(*stored(("M", c, 3)))
                            pe.wait_ge(s_T0, first_merges.index(c) + 1)
                        else:
                            pe.wait_ge(*stored((rhs, c, n - 1)))
                    else:
                        pe.wait_ge(s_bd, bd_count(c, n - 1))
                        pe.wait_ge(*stored((rhs, c, n)))
                    for p_ in range(NP):
                        ins = M(bank[:, p_ * 64:(p_ + 1) * 64], s[lhs][:, p_, :], s[rhs][:, p_, :],
                                start=True, stop=True)
                elif kind == "P":
                    pe.wait_ge(*stored(("Q", c, 3)))
                    for hd in range(NH):
                        r, p_ = 64 * (hd % 2), hd // 2
                        ins = M(bank[r:r + 64, p_ * 64:(p_ + 1) * 64], Qm[c % 2][:, hd, 0:64], UV[:, c, hd, :],
                                start=True, stop=True)
                elif kind == "X":
                    pe.wait_ge(*stored(("S", c - 1, 0)))
                    for hd in range(NH):
                        r, p_ = 64 * (hd % 2), hd // 2
                        ins = M(bank[r:r + 64, p_ * 64:(p_ + 1) * 64], AR[:, p_, c, 0, :],
                                bdS[c % 2][:, p_, r:r + 64], start=True, stop=True)
                elif kind == "U":
                    up = 64 * (1 - c % 2)
                    if n == 0:
                        pe.wait_ge(s_bd, bd_count(c, LEVELS - 1))
                        pe.wait_ge(*stored(("X" if c else "P", c, 0)))
                    for q in range(8):
                        hd = 8 * n + q
                        ins = M(bank[up:up + 64, q * 64:(q + 1) * 64],
                                s["bdTT"][:, hd // 2, 64 * (hd % 2):64 * (hd % 2) + 64], Xst[:, hd // 2, :],
                                start=True, stop=True)
                elif kind == "S":
                    pe.wait_ge(*stored(("U", c, 0)))
                    pe.wait_ge(*stored(("U", c, 1)))
                    for hd in range(NH):
                        r, p_ = 64 * (hd % 2), hd // 2
                        ins = M(bank[r:r + 64, p_ * 64:(p_ + 1) * 64], BKT[:, p_, c, r:r + 64], UV[:, c, hd, :],
                                start=True, stop=True)
                elif kind == "Y":
                    if c == NC - 1:
                        pe.wait_ge(*stored(("U", c, 0)))
                        pe.wait_ge(*stored(("U", c, 1)))
                    r0 = 64 * (c % 2)
                    for q in range(4):
                        p_ = 4 * n + q
                        if c > 0:
                            M(bank[r0:r0 + 64, q * P:(q + 1) * P], AR[:, p_, c, 1, :], bdS[c % 2][:, p_, :],
                              start=True, stop=False, skip_group_check=True)
                        for i2 in range(2):
                            ins = M(bank[r0:r0 + 64, q * P + 64 * i2:q * P + 64 * i2 + 64],
                                    Qm[c % 2][:, 2 * p_ + i2, 64:128], UV[:, c, 2 * p_ + i2, :],
                                    start=(c == 0), stop=True, skip_group_check=True)
                elif kind == "G":
                    t, half = c // 2, c % 2
                    pe.wait_ge(s_yg, t + 1)
                    yf = yS[:, t].rearrange("p h v -> p (h v)")
                    for q in range(4):
                        k = 4 * half + q
                        ins = nc.tensor.transpose(bank[:, q * P:(q + 1) * P], yf[:, k * P:(k + 1) * P], ident)
                ins.then_inc(s_job, 1)
            pe.wait_ge(s_ygT, 4)
            for q in range(4):
                c, t = q // 2, q % 2
                w = arrived(8 + c).rearrange("p (k n) -> p k n", k=KT)
                for k in range(KT):
                    ins = M(ps[:, 4 + q, :], ygT[:, k, t * P:(t + 1) * P], w[:, k, :], start=(k == 0),
                            stop=(k == KT - 1))
                ins.then_inc(s_acc, 1)

            def ring_slot(i):
                pe.wait_ge(s_w[i % RING], 16 * (i // RING + 1))
                return slot(i % RING)

            transposes(1)
            u_ready(1)
            for f in range(FT):
                if f % 2 == 0:
                    w = ring_slot(f // 2).rearrange("p (k g n) -> p k g n", k=KT, g=4)
                if f >= 4:
                    pe.wait_ge(s_fa, f - 3)
                for i in range(2):
                    for k in range(KT):
                        ins = M(ps[:, f % 4, i * T:(i + 1) * T], w[:, k, 2 * (f % 2) + i, :], uT[:, k, :],
                                start=(k == 0), stop=(k == KT - 1))
                ins.then_inc(s_fh, 1)
                if f % 2:
                    owed.append(s_free)
            for f in range(FT):
                if f % 4 == 0:
                    w = ring_slot(FT // 2 + f // 4)
                pe.wait_ge(s_fa, f + 1)
                for q in range(4):
                    c, t = q // 2, q % 2
                    ins = M(ps[:, 4 + q, :], hT[:, f, t * P:(t + 1) * P],
                            w[:, (f % 4) * D + c * 512:(f % 4) * D + (c + 1) * 512],
                            start=(f == 0), stop=(f == FT - 1), skip_group_check=True)
                    if f == FT - 1:
                        ins.then_inc(s_acc, 1)
                if f == FT - 1:
                    owed.append(s_free)
                elif f % 4 == 3:
                    ins.then_inc(s_free, 1)

            transposes(2)
            u_ready(2)
            for j in rjobs:
                kind, i, who = j
                n = rnum[j[:2]]
                bank = ps[:, n % 8, :]
                if n >= 8:
                    pe.wait_ge(*rstored(rjobs[n - 8][:2]))
                if kind in "qk":
                    w = ring_slot(F_SLOTS + 2 * (kind == "k") + i // 2).rearrange("p (k n) -> p k n", k=KT)
                    for y in range(2):
                        c0 = (i % 2) * 256 + y * P
                        for k in range(KT):
                            ins = M(bank[:, y * T:(y + 1) * T], w[:, k, c0:c0 + P], uT[:, k, :],
                                    start=(k == 0), stop=(k == KT - 1))
                    if i % 2:
                        owed.append(s_free)
                elif kind in "vg":
                    w = ring_slot(F_SLOTS + 4 + 4 * (kind == "g") + i // 2).rearrange("p (k n) -> p k n", k=KT)
                    t = i % 2
                    for k in range(KT):
                        ins = M(bank, uT[:, k, t * P:(t + 1) * P], w[:, k, :], start=(k == 0), stop=(k == KT - 1))
                    if t:
                        owed.append(s_free)
                elif kind == "s":
                    pe.wait_ge(*rstored(("k", i)))
                    for y in range(2):
                        M(bank[:, 0:256], kTr[:, i, y, 0:P], qTr[:, i, y, :], start=(y == 0), stop=(y == 1))
                    for y in range(2):
                        ins = M(bank[:, 256:384], kTr[:, i, y, P:T], qTr[:, i, y, P:T], start=(y == 0), stop=(y == 1))
                elif kind == "o":
                    hd, t = i // 2, i % 2
                    if i == 0:
                        pe.wait_ge(*rstored(("s", RH - 1)))
                        pe.wait_ge(*rstored(("v", 7)))
                    for c in range(2):
                        cs = slice(c * 256, (c + 1) * 256)
                        vs = slice(hd * RV + c * 256, hd * RV + (c + 1) * 256)
                        ins = M(bank[:, cs], ST[:, hd, t * P:(t + 1) * P], vtok[:, 0, vs], start=True, stop=(t == 0))
                        if t:
                            ins = M(bank[:, cs], ST[:, hd, 256:384], vtok[:, 1, vs], start=False, stop=True)
                else:
                    t, kg = i // 4, i % 4
                    if i == 0:
                        pe.wait_ge(*rstored(("o", 7)))
                    for q in range(4):
                        k = 4 * kg + q
                        ins = nc.tensor.transpose(bank[:, q * P:(q + 1) * P], og[:, t, k * P:(k + 1) * P], ident)
                ins.then_inc(s_rj, 1)
            pe.wait_ge(*rstored(("t", 6)))
            pe.wait_ge(*rstored(("t", 7)))
            for k in range(16):
                if k % 4 == 0:
                    w = ring_slot(F_SLOTS + 12 + k // 4)
                for q in range(4):
                    c, t = q // 2, q % 2
                    ins = M(ps[:, 4 + q, :], ogT[:, k, t * P:(t + 1) * P],
                            w[:, (k % 4) * D + c * 512:(k % 4) * D + (c + 1) * 512],
                            start=(k == 0), stop=(k == 15), skip_group_check=True)
                    if k == 15:
                        ins.then_inc(s_acc, 1)
                if k == 15:
                    owed.append(s_free)
                elif k % 4 == 3:
                    ins.then_inc(s_free, 1)

            transposes(3)
            u_ready(3)
            for t in range(TT):
                for k in range(KT):
                    ins = M(ps[:, 7, 8 * t:8 * t + 8], uT[:, k, t * P:(t + 1) * P],
                            par[:, P_ROUTER + 8 * k:P_ROUTER + 8 * k + 8], start=(k == 0), stop=(k == KT - 1))
            ins.then_inc(s_lg, 1)
            pe.wait_ge(s_ms2, 1)
            tri = cst[:, C_TRI:C_TRI + P]
            m0, m1 = rw(96, 8), rw(104, 8)
            M(ps[:, 7, 32:40], tri, m0, start=True, stop=True)
            M(ps[:, 7, 40:48], ones, m0, start=True, stop=False)
            M(ps[:, 7, 40:48], tri, m1, start=False, stop=True)
            M(ps[:, 7, 48:56], ones, m0, start=True, stop=False)
            M(ps[:, 7, 48:56], ones, m1, start=False, stop=True).then_inc(s_cum, 1)

            pe.wait_ge(s_tabr, 1)
            extras = pe.value_load(itab[0:1, 0:1], min_val=0, max_val=EXTRA)
            with pe.Fori(0, extras + NE) as e:
                def moe_slot(i):
                    n = PRE + i
                    pe.wait_ge(s_w[n % RING], e * (16 * E_SLOTS // RING) + 16 * (n // RING + 1))
                    return slot(n % RING)

                pe.wait_ge(s_oh, e * 2 + 2)
                for g in range(2):
                    for q in range(4):
                        k = 4 * g + q
                        for t in range(TT):
                            ins = M(ps[:, 7 - g, q * P:(q + 1) * P], xn[:, t, k * P:(k + 1) * P], oh[:, t, :],
                                    start=(t == 0), stop=(t == TT - 1))
                    ins.then_inc(s_gp, 1)
                pe.wait_ge(s_ga, e * 9 + 1)
                for t in range(TT):
                    ins = nc.tensor.transpose(ps[:, 7, t * P:(t + 1) * P], ohg[:, t, :], ident)
                ins.then_inc(s_gp, 1)
                pe.wait_ge(s_ga, e * 9 + 2)
                n_slot = 0
                for j in range(FJ + 1):
                    if j < FJ:
                        if j >= 2:
                            pe.wait_ge(s_ma, e * FJ + (j - 1))
                        for i in range(2):
                            w = moe_slot(n_slot).rearrange("p (k n) -> p k n", k=KT)
                            n_slot += 1
                            for k in range(KT):
                                ins = M(ps[:, 2 * (j % 2) + i, :], xeT[:, 0, k, :], w[:, k, :], start=(k == 0),
                                        stop=(k == KT - 1))
                            if i == 0:
                                ins.then_inc(s_free, 1)
                        ins.then_inc(s_mh, 1)
                        owed.append(s_free)
                    if j >= 1:
                        i = j - 1
                        pe.wait_ge(s_ma, e * FJ + j)
                        if i == 1:
                            pe.wait_ge(s_gd, e * 5 + 1)
                        elif i >= 2:
                            pe.wait_ge(s_ga, e * 9 + (1 + i))
                        for g in range(4):
                            ins = nc.tensor.transpose(ps[:, 7 - (3 + i) % 2, g * P:(g + 1) * P],
                                                      act[:, i % 2, g * P:(g + 1) * P], ident)
                            if owed:
                                ins.then_inc(owed.pop(), 1)
                        ins.then_inc(s_gp, 1)
                        w = moe_slot(n_slot)
                        n_slot += 1
                        pe.wait_ge(s_ga, e * 9 + (3 + i))
                        for g in range(4):
                            for c in range(2):
                                ins = M(ps[:, 4 + c, :], actT[:, i % 2, g, :],
                                        w[:, g * D + c * 512:g * D + (c + 1) * 512],
                                        start=(i == 0 and g == 0), stop=(i == FJ - 1 and g == 3),
                                        skip_group_check=True)
                        if i < FJ - 1:
                            ins.then_inc(s_free, 1)
                ins.then_inc(s_y, 1)
                owed.append(s_free)
                pe.wait_ge(s_ye, e + 1)
                for q in range(4):
                    t, c = q // 2, q % 2
                    if q == 0:
                        pe.wait_ge(s_gd, e * 5 + 1)
                    if q >= 2:
                        pe.wait_ge(s_gd, e * 5 + q)
                    for i in range(2):
                        ins = M(ps[:, 7 - q % 2, i * 256:(i + 1) * 256], ohT[:, t * P:(t + 1) * P],
                                ysb[:, c * 512 + i * 256:c * 512 + (i + 1) * 256], start=True, stop=True)
                    ins.then_inc(s_gp, 1)


def kernel(**inputs):
    import concourse.bacc as _bacc
    from concourse.bass_utils import run_bass_kernel_spmd as _run

    g = {k: np.asarray(v) for k, v in inputs.items()}

    def cols(w, n=512):
        k_, n_ = w.shape
        return w.reshape(k_ // P, P, n_ // n, n).transpose(2, 1, 0, 3).reshape(n_ // n, P, k_ // P * n)

    def rows_of(w):
        return w.reshape(-1, 4, P, D).transpose(0, 2, 1, 3).reshape(-1, P, 4 * D)

    lora = np.zeros((2, P, SLOT), np.float32)
    first = np.concatenate([g["a_w1"][0], g["a_a1"][0], g["a_g1"][0]], axis=1)
    lora[0, :, :KT * 288] = cols(first, 288)[0]
    lora[0, :64, KT * 288:KT * 288 + D] = g["a_w2"][0]
    lora[0, 64:, KT * 288:KT * 288 + D] = g["a_a2"][0]
    lora[1, :, :D] = g["a_g2"][0, :P]
    lora[1, :32, D:2 * D] = g["a_g2"][0, P:]
    rstream = np.concatenate([lora] + [cols(g[n][0]) for n in ("a_wk", "a_wr", "a_wv", "a_wo")])
    w13 = np.stack([g["f_w1"][0].reshape(KT, P, FT // 2, 2, P), g["f_w3"][0].reshape(KT, P, FT // 2, 2, P)], axis=4)
    w13 = w13.transpose(2, 1, 0, 3, 4, 5).reshape(FT // 2, P, SLOT)
    w2 = np.zeros((6 * 512, D), np.float32)
    w2[:FF] = g["f_w2"][0]

    def parity(w):
        return w.reshape(D, RH, RK // 2, 2).transpose(0, 1, 3, 2).reshape(D, D)

    pstream = np.concatenate([w13, rows_of(w2), cols(parity(g["b_wq"][0])), cols(parity(g["b_wk"][0])),
                              cols(g["b_wv"][0]), cols(g["b_wg"][0]), rows_of(g["b_wo"][0])])
    mstream = np.empty((NE, E_SLOTS, P, SLOT), np.float32)
    at1 = [0, 2] + [5 + 3 * i for i in range(FJ - 2)]
    at2 = [4 + 3 * i for i in range(FJ - 1)] + [E_SLOTS - 1]
    for e in range(NE):
        mstream[e, at1] = cols(g["m_w1"][0, e])
        mstream[e, [i + 1 for i in at1]] = cols(g["m_w3"][0, e])
        mstream[e, at2] = rows_of(g["m_w2"][0, e])
    mstream = mstream.reshape(NE * E_SLOTS, P, SLOT)

    vecs = np.concatenate([g["norm_mix"][0:1], g["norm_ffn"][0:1], g["norm_mix"][1:2], g["norm_ffn"][1:2],
                           g["a_mu"][0], g["a_w0"], g["a_a0"], g["a_kk"], g["a_ka"], g["a_rk"].reshape(1, D)])
    params = np.concatenate([vecs.reshape(15, KT, P).transpose(2, 0, 1).reshape(P, 15 * KT),
                             g["m_router"][0].reshape(KT, P, NE).transpose(1, 0, 2).reshape(P, KT * NE)], axis=1)
    rows = np.concatenate([g["a_gn_w"], g["a_gn_b"], g["norm_final"][None]])
    consts, qconsts, tabs = const_tables()
    arrays = {"x": g["x"].reshape(TT, P, D).transpose(1, 0, 2), "consts": consts, "qconsts": qconsts, "tabs": tabs,
              "params": params, "rows": rows, "rstream": rstream, "pstream": pstream, "mstream": mstream}
    arrays = {k: np.ascontiguousarray(v) for k, v in arrays.items()}
    nc = _bacc.Bacc("TRN2", target_bir_lowering=False, num_devices=1)
    aps = [nc.dram_tensor(k, v.shape, mybir.dt.from_np(v.dtype), kind="ExternalInput").ap() for k, v in arrays.items()]
    out = nc.dram_tensor("out", (P, TT, D), F32, kind="ExternalOutput").ap()
    build(nc, *aps, out)
    r = _run(nc, [arrays], core_ids=[0])
    return r.results[0]["out"].reshape(P, TT, D).transpose(1, 0, 2).reshape(1, T, D)
```

```python
import math
from contextlib import ExitStack

import numpy as np
import concourse.bass as bass
from concourse import mybir

F32 = mybir.dt.float32
F32R = mybir.dt.float32r
I32 = mybir.dt.int32
ALU = mybir.AluOpType
ACT = mybir.ActivationFunctionType
AX = mybir.AxisListType

P = 128
D = 1024
T = 256
KT = D // P
TT = T // P
EPS = 1e-6
GN_EPS = 64e-5
NH, HN = 16, 64
NP = NH // 2
CH = 64
NC = T // CH
LEVELS = 6
FF = 2816
FT = FF // P
RH, RK, RV = 4, 256, 512
NE = 8
FE = 3584
FJ = FE // 512
SLOT = 4096
R_SLOTS = 10
UNIT = 2048
RING = 6
PAIRS, M_PAIRS = 3, 6
U_W2 = FT
U_Q = U_W2 + FT // 2
U_K = U_Q + RH
U_V = U_K + RH
U_G = U_V + 8
U_O = U_G + 8
PRE = U_O + 8
E_UNITS = 6 * FJ
FIRST = 4
EXTRA = 3
NI = NE + EXTRA
assert E_UNITS % RING == 0 and E_UNITS % M_PAIRS == 0

C_ID, C_ONE, C_TRI, C_IOTA, C_TIE, C_EIDX = 0, 128, 256, 384, 512, 576
C_COLS = 592
(V_NM0, V_NF0, V_NM1, V_NF1, V_MU, V_W0, V_A0, V_KK, V_KA, V_RK) = (0, 1, 2, 3, 4, 10, 11, 12, 13, 14)
P_ROUTER = 15 * KT
P_COLS = P_ROUTER + KT * NE
Q_BO, Q_MASK, Q_SEL, Q_ML, Q_MU, Q_EYE, Q_LEV = 0, 128, 256, 258, 322, 386, 450
Q_COLS = Q_LEV + 2 * LEVELS * 64


def const_tables():
    i = np.arange(P)
    c = np.zeros((P, C_COLS), np.float32)
    c[:, C_ID:C_ID + P] = np.eye(P)
    c[:, C_ONE:C_ONE + P] = 1
    c[:, C_TRI:C_TRI + P] = i[:, None] <= i[None, :]
    c[:, C_IOTA:C_IOTA + P] = i[None, :] + 1
    e = np.arange(NE)
    c[:, C_TIE:C_TIE + 64] = (e[None, :] < e[:, None]).reshape(-1)
    c[:, C_EIDX:C_EIDX + NE] = e
    q = np.zeros((P, Q_COLS), np.float32)
    q[:, Q_BO:Q_BO + P] = (i[:, None] // 64) == (i[None, :] // 64)
    s, t = i[:, None] % 64, i[None, :] % 64
    q[:, Q_MASK:Q_MASK + P] = np.where(i[None, :] < 64, s < t, s <= t)
    q[:, Q_SEL:Q_SEL + 2] = (i[:, None] // 64) == np.arange(2)[None, :]
    r, k = i[:, None] % 64, np.arange(64)[None, :]
    q[:, Q_ML:Q_ML + 64] = r > k
    q[:, Q_MU:Q_MU + 64] = r < k
    q[:, Q_EYE:Q_EYE + 64] = r == k
    for lv in range(LEVELS):
        b = 2 << lv
        same = (r // b) == (k // b)
        low = same & (r % b >= b // 2) & (k % b < b // 2)
        up = same & (k % b >= b // 2) & (r % b < b // 2)
        q[:, Q_LEV + 128 * lv:Q_LEV + 128 * lv + 64] = low
        q[:, Q_LEV + 128 * lv + 64:Q_LEV + 128 * lv + 128] = up
    f32 = np.float32
    angle = (f32(1.0) / (f32(10000.0) ** np.linspace(0, 1, RK // 2, dtype=f32))).astype(f32)
    ang = (angle[:, None] * np.arange(T, dtype=f32)[None, :]).astype(f32)
    tab = np.zeros((P, 2 * T + RH * 384), f32)
    tab[:, 0:T] = np.cos(ang.astype(np.float64))
    tab[:, T:2 * T] = np.sin(ang.astype(np.float64))
    for h in range(RH):
        lg = math.log(1.0 - 2.0 ** (-5.0 - h))
        for m0, c0, n, at in ((0, 0, 256, 0), (128, 128, 128, 256)):
            dif = (c0 + np.arange(n))[None, :] - (m0 + i)[:, None]
            tab[:, 2 * T + 384 * h + at:2 * T + 384 * h + at + n] = np.where(
                dif >= 0, np.exp(lg * np.maximum(dif, 0)) * RK ** -0.5, 0)
    return c, q, tab


def build(nc, x, consts, qconsts, tabs, params, rows, rstream, pstream, mstream, out):
    ctx = ExitStack()
    with ctx:
        def sb(name, cols, dt=F32):
            return ctx.enter_context(nc.sbuf_tensor(name, [P, cols], dt))

        def sem(name):
            return ctx.enter_context(nc.semaphore(name))

        PAIR_COLS, WORK = PAIRS * 2 * UNIT, 25088
        with nc.sbuf_tensor("mem", [P, RING * UNIT + PAIR_COLS + WORK], F32) as mem:
            pass
        ring = sb("ring", RING * UNIT)
        pairs_r = sb("pairs_r", PAIR_COLS, F32R)
        with nc.sbuf_tensor("work", [P, WORK], F32) as work:
            pass
        workr = sb("workr", WORK, F32R)
        h = sb("h", TT * D)
        cst = sb("cst", C_COLS)
        par = sb("par", P_COLS)
        small = sb("small", 256)
        route = sb("route", 384)
        itab = sb("itab", 8, I32)
        ps = ctx.enter_context(nc.psum_tensor("ps", [P, 8, 512], F32))

        def slot(p):
            return mem[:, p * SLOT:(p + 1) * SLOT]

        def unit(i):
            p = (i + FIRST) % RING
            return ring[:, p * UNIT:(p + 1) * UNIT]

        def pair(i):
            n = i % (M_PAIRS if i >= PRE else PAIRS)
            base, at = (pairs_r, n * 2 * UNIT) if n < PAIRS else (workr, 12288 + (n - PAIRS) * 2 * UNIT)
            return base[:, at:at + UNIT], base[:, at + UNIT:at + 2 * UNIT]

        def vec(v, k):
            return par[:, v * KT + k:v * KT + k + 1]

        hv = h[:, :].rearrange("p (t d) -> p t d", t=TT)
        ident = cst[:, C_ID:C_ID + P]
        ones = cst[:, C_ONE:C_ONE + P]

        def blk(n, count=1):
            return mem[:, 3 * SLOT + n * 2048:3 * SLOT + (n + count) * 2048]

        def fm(a):
            return a.rearrange("p (k t) -> p k t", k=KT)

        uT_r, dxT = fm(blk(0)), fm(blk(1))
        mix = [fm(blk(2)), fm(blk(3))]
        kT, rT, aT = blk(4), blk(5), blk(6)
        dT, d1T, gT, giT = blk(7), blk(8), blk(11), blk(7)
        sqT, kkT, kmT = blk(8), blk(9), blk(10)
        BK = blk(0, 2).rearrange("p (n c x t) -> p n c x t", n=NP, c=NC, x=2)
        BKT = blk(2, 2).rearrange("p (n c k) -> p n c k", n=NP, c=NC)
        BKh = blk(8, 2).rearrange("p (n c k) -> p n c k", n=NP, c=NC)
        UV = blk(12, 2).rearrange("p (c h v) -> p c h v", c=NC, h=NH)
        gtok = blk(14).rearrange("p (t d) -> p t d", t=TT)
        vtok_r = blk(15).rearrange("p (t d) -> p t d", t=TT)
        AR = blk(16, 2).rearrange("p (n c x t) -> p n c x t", n=NP, c=NC, x=2)
        ygT = fm(blk(16))
        Qm = [blk(4 + i).rearrange("p (h t) -> p h t", h=NH) for i in range(2)]
        sets = []
        for a, b, c in ((6, 7, 11), (8, 9, 10)):
            bd = [v.rearrange("p (x n s) -> p x n s", x=2, n=NP) for v in (blk(a), blk(b))]
            st = blk(c).rearrange("p (x n s) -> p x n s", x=4, n=NP)
            sets.append(dict(bdM=bd[0][:, 0], bdMT=bd[0][:, 1], bdT=bd[1][:, 0], bdTT=bd[1][:, 1],
                             T=st[:, 0], TT=st[:, 1], W=st[:, 2], WT=st[:, 3], bds=(blk(a), blk(b))))
        qc = mem[:, 2 * SLOT:2 * SLOT + Q_COLS]
        gnw = mem[:, 2 * SLOT + 1280:2 * SLOT + 2304]
        gnb = mem[:, 2 * SLOT + 2304:2 * SLOT + 3328]
        Xst = mem[:, 2 * SLOT + 3328:2 * SLOT + 3840].rearrange("p (n v) -> p n v", n=NP)
        assert Q_COLS <= 1280
        yS = mem[:, SLOT:SLOT + 2048].rearrange("p (t h v) -> p t h v", t=TT, h=NH)
        bdS = [mem[:, SLOT + 2048 + 1024 * i:SLOT + 3072 + 1024 * i].rearrange(
            "p (n v) -> p n v", n=NP) for i in range(2)]
        lora_sb = blk(16)
        lor, sg1, sg2 = lora_sb[:, 0:T], lora_sb[:, T:2 * T], lora_sb[0:32, 2 * T:3 * T]
        gC = small[:, 64:96]
        bon = small[:, 96:128].rearrange("p (t h) -> p t h", t=TT)
        gsum = small[:, 128:144]
        gvar = small[:, 144:160]
        gsd = small[:, 160:176]
        ss = small[:, 0:16]
        sd = small[:, 16:32]
        rstd = small[:, 32:48]

        def wk(a, n, dims="", base=work, **sizes):
            v = base[:, a:a + n]
            return v.rearrange(f"p ({dims}) -> p {dims}", **sizes) if dims else v

        xn0 = blk(8).rearrange("p (t d) -> p t d", t=TT)
        xn_ = wk(0, 2048, "t d", t=TT)
        uTh, uTl = (wk(a, 2048, "k t", workr, k=KT) for a in (2048, 4096))
        hTh, hTl = (wk(a, FT * T, "f t", workr, f=FT) for a in (6144, 6144 + FT * T))
        sl = wk(17408, 512, "b t", b=2)
        a32 = wk(17920, 512, "b t", b=2)
        qTr = wk(6144, 2048, "h x t", h=RH, x=2)
        kTr = wk(8192, 2048, "h x t", h=RH, x=2)
        ogTh, ogTl = (wk(a, 4096, "k t", workr, k=16) for a in (2048, 6144))
        vtok = wk(10240, 4096, "t d", t=TT)
        og = wk(14336, 4096, "t d", t=TT)
        tab = wk(18432, 2048)
        ST = wk(20480, 1536, "h c", h=RH)
        rot = wk(0, 1024, "y x t", y=2, x=2)
        osq = wk(1024, 512)
        rss = small[:, 48:56]
        rsd = small[:, 56:64]
        rrs = small[:, 176:184]
        uT3 = wk(2048, 2048, "k t", k=KT)
        s1 = wk(2048, 1024, "b f", b=2)
        act = wk(3072, 1024, "b f", b=2)
        gfin = wk(4096, 1024)
        xeTh, xeTl = (wk(a, 1024, "k s", workr, k=KT) for a in (5120, 6144))
        oh = wk(7168, 256, "t s", t=TT)
        ohg = wk(7424, 256, "t s", t=TT)
        ohT = wk(7680, 256)
        actTh, actTl = (wk(a, 1024, "b g s", workr, b=2, g=4) for a in (8192, 9216))
        ysb = wk(10240, 1024)
        junk = wk(11264, 1024)
        rw = lambda a, n: route[:, a:a + n]

        s_x = sem("x_loaded")
        s_c = sem("tables_loaded")
        s_q = sem("rwkv_tables_loaded")
        s_tab = sem("retention_tables_loaded")
        s_gf = sem("final_gain_loaded")
        s_ra = [sem(f"rwkv_weights_{i}") for i in range(2)]
        s_w = [sem(f"weights_{i}") for i in range(RING)]
        s_hi = sem("high_parts_ready")
        s_lo = sem("low_parts_ready")
        s_pu = sem("pairs_used")
        s_ss = sem("squares_summed")
        s_ms = sem("mean_square_ready")
        s_sd = sem("root_ready")
        s_rs = sem("rstd_ready")
        s_xn = sem("normed_ready")
        s_nt = sem("norm_transposed")
        s_uTa = sem("uT_by_scalar")
        s_uTd = sem("uT_by_vector")
        s_h = sem("residual_updated")
        d_step = sem("vector_step")
        a_step = sem("scalar_step")
        p_step = sem("pool_step")
        s_mix = sem("mix_ready")
        s_pj = sem("projection_ready")
        s_pe = sem("projection_stored")
        s_d = sem("decay_ready")
        s_kkr = sem("kk_raw_ready")
        s_sq = sem("kk_squared")
        s_nrm = sem("kk_norm_ready")
        s_pz = sem("pool_zeroed")
        s_g = sem("cumulated_decay_ready")
        s_BK = sem("BK_ready")
        s_AR = sem("AR_ready")
        s_BKh = sem("BKhat_ready")
        s_z = sem("bonus_products_ready")
        s_uv = sem("V_in_place")
        s_cb = sem("gate_terms_ready")
        s_job = sem("core_bank_ready")
        s_jd = sem("core_stored_by_vector")
        s_ja = sem("core_stored_by_scalar")
        s_bd = sem("block_diagonals_ready")
        s_zset = sem("inverse_buffers_zeroed")
        s_T0 = sem("first_merge_ready")
        s_gv = sem("group_variance_ready")
        s_gs = sem("group_root_ready")
        s_yg = sem("gated_y_ready")
        s_ygt = sem("gated_y_transposed")
        s_ygT = sem("ygT_ready")
        s_acc = sem("block_output_ready")
        s_fh = sem("ffn_hidden_ready")
        s_fs = sem("ffn_silu_ready")
        s_fa = sem("ffn_act_ready")
        s_fah = sem("ffn_act_high_ready")
        s_fal = sem("ffn_act_low_ready")
        s_rj = sem("retention_bank_ready")
        s_rd = sem("retention_stored_by_vector")
        s_rA = sem("retention_stored_by_scalar")
        s_oss = sem("o_squares_ready")
        s_om = sem("o_mean_square_ready")
        s_or = sem("o_root_ready")
        s_lg = sem("logits_ready")
        s_ms2 = sem("masks_ready")
        s_cum = sem("positions_ready")
        s_dt = sem("gate_difference_ready")
        s_de = sem("gate_exp_ready")
        s_tabr = sem("routing_ready")
        s_key = sem("places_and_gates_copied")
        s_oh = sem("one_hot_ready")
        s_xg = sem("tokens_gathered")
        s_xh = sem("gathered_high_parts_ready")
        s_xl = sem("gathered_low_parts_ready")
        s_gp = sem("moe_small_bank_ready")
        s_gd = sem("moe_small_stored")
        s_ga = sem("moe_act_high_parts_ready")
        s_w1 = sem("moe_w1_product_ready")
        s_w3 = sem("moe_w3_product_ready")
        s_m1 = sem("moe_silu_ready")
        s_ma = sem("moe_act_ready")
        s_ye = sem("expert_output_stored")
        s_fin = sem("final_ready")
        s_out = sem("output_written")

        J_T1, J_G1, J_W, J_A, J_G, J_K, J_R, J_SS, J_V = 0, 1, 2, 6, 10, 14, 18, 22, 26
        def inverse_jobs(c):
            js = [("Q", c, i) for i in range(4)] + [("M", c, i) for i in range(4)]
            for lv in range(1, LEVELS):
                if lv < LEVELS - 1:
                    js += [("W", c, lv), ("WT", c, lv), ("T", c, lv), ("TT", c, lv)]
                else:
                    js += [("WT", c, lv), ("TT", c, lv)]
            return js

        def chain_jobs(c):
            return ([("P", c, 0)] + [("X", c, 0)] * (c > 0) + [("U", c, 0), ("U", c, 1)]
                    + [("S", c, 0)] * (c < NC - 1) + [("Y", c, 0), ("Y", c, 1)])

        def zipped(a, b):
            o = []
            for i in range(max(len(a), len(b))):
                o += a[i:i + 1] + b[i:i + 1]
            return o

        jobs = [("B", i, 0) for i in range(8)] + [("Z", 0, 0)]
        jobs += zipped(inverse_jobs(0), inverse_jobs(1)) + chain_jobs(0)
        jobs += zipped(inverse_jobs(2), chain_jobs(1)) + zipped(inverse_jobs(3), chain_jobs(2)) + chain_jobs(3)
        jobs += [("G", i, 0) for i in range(4)]
        by_act = {"B", "P", "Y", "G"}

        def stored_by(job):
            kind, _, n = job
            return "a" if kind in by_act or (kind == "U" and n == 0) else "d"

        number = {j: n for n, j in enumerate(jobs)}
        count = {}
        for who in "ad":
            seen = 0
            for j in jobs:
                if stored_by(j) == who:
                    seen += 1
                    count[j] = seen

        def stored(job):
            return (s_ja if stored_by(job) == "a" else s_jd), count[job]

        def made(job):
            return s_job, number[job] + 1

        def bd_count(c, lv):
            order = [j for j in jobs if j[0] == "TT" or (j[0], j[2]) == ("M", 3)]
            key = ("M", c, 3) if lv == 0 else ("TT", c, lv)
            return order.index(key) + 1

        first_merges = [j[1] for j in jobs if (j[0], j[2]) == ("M", 3)]

        rjobs = [("q", i, "d") for i in range(RH)] + [("k", i, "d") for i in range(RH)]
        rjobs += [("s", i, "d") for i in range(RH)] + [("v", i, "a") for i in range(8)] + [("g", i, "a") for i in range(8)]
        rjobs += [("o", i, "d") for i in range(8)] + [("t", i, "d") for i in range(8)]
        rnum = {j[:2]: n for n, j in enumerate(rjobs)}
        rcount = {}
        for who in "ad":
            mine = [j for j in rjobs if j[2] == who]
            rcount.update({j[:2]: n + 1 for n, j in enumerate(mine)})
        rstores_a = rcount[("g", 7)]
        rwho = {j[:2]: j[2] for j in rjobs}

        def rstored(job):
            return (s_rA if rwho[job] == "a" else s_rd), rcount[job]

        def first_unit(j):
            return 6 * j - 2 if j else 0

        SMALL = 5 + FJ
        N_OT, N_ACT = 5, 6
        BACK = (7, 6, 5, 4)

        block = ctx.enter_context(nc.Block())

        @block.sync
        def _(sp):
            sp.dma_start(h[:, :].rearrange("p (t d) -> p t d", t=TT), x).then_inc(s_x, 16)
            used_after = {2: J_A + 4, 3: J_G + 4, 4: J_K + 2, 5: J_K + 4, 6: J_R + 2, 7: J_R + 4, 8: J_V + 2, 9: J_V + 4}
            for i in range(R_SLOTS):
                if i >= 2:
                    sp.wait_ge(s_pj, used_after[i])
                if i == R_SLOTS - 1:
                    sp.wait_ge(s_ygT, 4)
                sp.dma_start(slot(i % 2), rstream[i]).then_inc(s_ra[i % 2], 16)
            for i in range(RING):
                if i in (2, 4):
                    sp.wait_ge(s_acc, i)
                sp.dma_start(unit(i), pstream[i]).then_inc(s_w[i % RING], 16)
            peeled = (PRE - RING) % RING
            for i in range(RING, RING + peeled):
                sp.wait_ge(s_lo, i - RING + 1)
                sp.dma_start(unit(i), pstream[i]).then_inc(s_w[i % RING], 16)
            with sp.Fori(0, (PRE - RING - peeled) // RING) as g:
                for j in range(RING):
                    i = RING + peeled + j
                    sp.wait_ge(s_lo, g * RING + (i - RING + 1))
                    sp.dma_start(unit(i), pstream[bass.ds(g * RING + i, 1), :, :].rearrange(
                        "a p n -> p (a n)")).then_inc(s_w[i % RING], 16)
            with sp.Fori(0, NE * E_UNITS // RING) as g:
                for j in range(RING):
                    i = PRE + j
                    sp.wait_ge(s_lo, g * RING + (i - RING + 1))
                    sp.dma_start(unit(i), mstream[bass.ds(g * RING + j, 1), :, :].rearrange(
                        "a p n -> p (a n)")).then_inc(s_w[i % RING], 16)
            sp.wait_ge(s_tabr, 1)
            extras = sp.value_load(itab[0:1, 0:1], min_val=0, max_val=EXTRA)
            for n in range(EXTRA):
                with sp.If(extras > n):
                    e = sp.value_load(itab[0:1, n + 1:n + 2], min_val=0, max_val=NE - 1)
                    base = PRE + (NE + n) * E_UNITS
                    with sp.Fori(0, E_UNITS // RING) as g:
                        for j in range(RING):
                            i = base + j
                            sp.wait_ge(s_lo, g * RING + (i - RING + 1))
                            sp.dma_start(unit(i), mstream[bass.ds(e * E_UNITS + g * RING + j, 1), :, :]
                                         .rearrange("a p n -> p (a n)")).then_inc(s_w[i % RING], 16)
                with sp.Else():
                    sp.nop()
            sp.wait_ge(s_fin, TT)
            sp.dma_start(out, xn_).then_inc(s_out, 16)
            sp.wait_ge(s_out, 16)

        @block.gpsimd
        def _(pool):
            chain = [0]

            def link(ins):
                chain[0] += 1
                ins.then_inc(p_step, 1)
                pool.wait_ge(p_step, chain[0])

            nc.gpsimd.memset(blk(12, 2), 0.0).then_inc(s_pz, 1)
            pool.wait_ge(s_nt, 4)
            nc.gpsimd.memset(d1T, 0.0).then_inc(s_pz, 1)
            pool.wait_ge(s_pe, J_V + 4)
            pool.wait_ge(s_pz, 2)
            for c in range(NC):
                r0 = 64 * (c % 2)
                nc.gpsimd.tensor_copy(UV[r0:r0 + 64, c], vtok_r[r0:r0 + 64, c // 2, :].rearrange(
                    "p (h v) -> p h v", h=NH)).then_inc(s_uv, 1)
                pool.wait_ge(s_uv, c + 1)
            pool.wait_ge(s_BK, 4)
            pool.wait_ge(s_AR, 3)
            nc.gpsimd.memset(sets[0]["bds"][0], 0.0).then_inc(s_zset, 1)
            nc.gpsimd.memset(sets[0]["bds"][1], 0.0).then_inc(s_zset, 1)
            pool.wait_ge(s_job, 8)
            nc.gpsimd.memset(sets[1]["bds"][0], 0.0).then_inc(s_zset, 1)
            nc.gpsimd.memset(sets[1]["bds"][1], 0.0).then_inc(s_zset, 1)
            pool.wait_ge(s_pj, J_V + 4)
            nc.gpsimd.memset(mem[:, SLOT + 2048:2 * SLOT], 0.0).then_inc(s_zset, 1)
            pool.wait_ge(*stored(("Z", 0, 0)))
            pool.wait_ge(s_uv, NC)
            pool.wait_ge(s_q, 48)
            v4 = vtok_r.rearrange("p t (h v) -> p (t h) v", h=NH)
            link(nc.gpsimd.tensor_tensor(v4, v4, bon.rearrange("p t h -> p (t h)").unsqueeze(2).to_broadcast(
                [P, TT * NH, HN]), ALU.mult))
            link(nc.gpsimd.tensor_tensor(vtok_r, vtok_r, gnb.unsqueeze(1).to_broadcast([P, TT, D]), ALU.add))
            nc.gpsimd.tensor_tensor(vtok_r, vtok_r, gtok, ALU.mult).then_inc(s_cb, 1)
            nc.gpsimd.tensor_tensor(gtok, gtok, gnw.unsqueeze(1).to_broadcast([P, TT, D]), ALU.mult).then_inc(s_cb, 1)

        @block.scalar
        def _(a):
            a.dma_start(cst[:, :], consts).then_inc(s_c, 16)
            a.dma_start(par[:, :], params).then_inc(s_c, 16)
            a.dma_start(qc, qconsts).then_inc(s_q, 16)
            a.dma_start(gnw, rows[0:1, :].to_broadcast([P, D])).then_inc(s_q, 16)
            a.dma_start(gnb, rows[1:2, :].to_broadcast([P, D])).then_inc(s_q, 16)
            act_f = nc.scalar.activation

            def norm_squares(n):
                if n == 0:
                    a.wait_ge(s_x, 16)
                else:
                    a.wait_ge(s_h, 4 * n)
                for t in range(TT):
                    act_f((xn_ if n else xn0)[:, t, :], hv[:, t, :], ACT.Square,
                          accum_out=ss[:, 2 * n + t:2 * n + t + 1]).then_inc(s_ss, 1)
                a.wait_ge(s_ms, n + 1)
                act_f(sd[:, 2 * n:2 * n + 2], rstd[:, 2 * n:2 * n + 2], ACT.Sqrt).then_inc(s_sd, 1)

            def norm_gain(n, v, dst):
                a.wait_ge(s_nt, 4 * (n + 1))
                for k in (0, 1, 4, 5):
                    act_f(dst[:, k, :], ps[:, k // 2, (k % 2) * T:(k % 2 + 1) * T], ACT.Copy, scale=vec(v, k)).then_inc(s_uTa, 1)

            def norm_high(n, v):
                for k in range(KT):
                    if k % 2 == 0:
                        a.wait_ge(s_nt, 4 * n + k // 2 + 1)
                    act_f(uTh[:, k, :], ps[:, k // 2, (k % 2) * T:(k % 2 + 1) * T], ACT.Copy,
                          scale=vec(v, k)).then_inc(s_uTa, 1)

            def split(i):
                a.wait_ge(s_w[i % RING], 16 * (i // RING + 1))
                if i >= PAIRS:
                    a.wait_ge(s_pu, i - PAIRS + 1)
                act_f(pair(i)[0], unit(i), ACT.Copy).then_inc(s_hi, 1)

            a.wait_ge(s_c, 32)
            norm_squares(0)
            norm_gain(0, V_NM0, uT_r)

            def take(j):
                a.wait_ge(s_pj, j + 1)
                return ps[:, j % 8, :]

            b = take(J_T1)
            act_f(lor[0:64, :], b[0:64, 0:T], ACT.Tanh)
            act_f(lor[64:128, :], b[64:128, 0:T], ACT.Copy).then_inc(s_pe, 1)
            b = take(J_G1)
            act_f(sg1, b[:, 0:T], ACT.Sigmoid)
            act_f(sg2, b[0:32, T:2 * T], ACT.Sigmoid).then_inc(s_pe, 1)
            for base, dst, v in ((J_W, dT, V_W0), (J_A, aT, V_A0)):
                for q in range(4):
                    b = take(base + q)
                    for i in range(2):
                        k = 2 * q + i
                        ins = act_f(fm(dst)[:, k, :], b[:, i * T:(i + 1) * T], ACT.Sigmoid, bias=vec(v, k))
                    ins.then_inc(s_pe, 1)
            a.wait_ge(s_pe, J_A + 4)
            act_f(dT, dT, ACT.Exp, scale=-math.exp(-0.5)).then_inc(s_d, 1)
            for q in range(4):
                b = take(J_G + q)
                act_f(gtok[:, q % 2, (q // 2) * 512:(q // 2 + 1) * 512], b, ACT.Copy).then_inc(s_pe, 1)
            for base, dst in ((J_K, kT), (J_R, rT)):
                for q in range(4):
                    b = take(base + q)
                    act_f(dst[:, q * 512:(q + 1) * 512], b, ACT.Copy).then_inc(s_pe, 1)
                if base == J_K:
                    a.wait_ge(s_kkr, 1)
                    a.wait_ge(s_g, 1)
                    act_f(sqT, kkT, ACT.Square).then_inc(s_sq, 1)
            for q in range(4):
                b = take(J_SS + q)
                act_f(sqT[:, q * 512:(q + 1) * 512], b, ACT.Sqrt).then_inc(s_pe, 1)
            for q in range(4):
                b = take(J_V + q)
                act_f(vtok_r[:, q % 2, (q // 2) * 512:(q // 2 + 1) * 512], b, ACT.Copy).then_inc(s_pe, 1)

            for j in jobs:
                kind, c, n = j
                bank = ps[:, number[j] % 8, :]
                up = 64 * (1 - c % 2)
                if stored_by(j) == "a":
                    a.wait_ge(*made(j))
                    if kind == "B":
                        act_f(BKT[:, c].rearrange("p c k -> p (c k)"), bank, ACT.Copy).then_inc(s_ja, 1)
                    elif kind == "P":
                        if c >= 1:
                            a.wait_ge(*made(("U", c - 1, 1)))
                        act_f(Xst.rearrange("p n v -> p (n v)"), bank, ACT.Copy).then_inc(s_ja, 1)
                    elif kind == "U":
                        act_f(UV[up:up + 64, c, 0:8, :].rearrange("p h v -> p (h v)"), bank[up:up + 64, :],
                              ACT.Copy).then_inc(s_ja, 1)
                    elif kind == "Y":
                        r0 = 64 * (c % 2)
                        act_f(yS[r0:r0 + 64, c // 2, 8 * n:8 * n + 8, :].rearrange("p h v -> p (h v)"),
                              bank[r0:r0 + 64, :], ACT.Copy).then_inc(s_ja, 1)
                        if n == 1 and c % 2:
                            a.wait_ge(s_gv, c // 2 + 1)
                            act_f(gsd, gvar, ACT.Sqrt).then_inc(s_gs, 1)
                    elif kind == "G":
                        t, half = c // 2, c % 2
                        act_f(ygT[:, 4 * half:4 * half + 4, t * P:(t + 1) * P],
                              bank.rearrange("p (k s) -> p k s", k=4), ACT.Copy).then_inc(s_ygT, 1)
                if (kind == "M" and n == 3) or (kind == "TT" and n < LEVELS):
                    s = sets[c % 2]
                    lv = 0 if kind == "M" else n
                    a.wait_ge(*made(j))
                    if lv == 0:
                        a.wait_ge(s_T0, first_merges.index(c) + 1)
                        a.wait_ge(s_zset, 2 + 2 * (c % 2))
                    else:
                        a.wait_ge(*stored(j))
                    for src, dst in (("T", "bdT"), ("TT", "bdTT")):
                        if lv == LEVELS - 1 and src == "T":
                            continue
                        for i in range(2):
                            r = slice(64 * i, 64 * i + 64)
                            ins = act_f(s[dst][r, :, r], s[src][r], ACT.Copy)
                    ins.then_inc(s_bd, 1)

            for i in range(PAIRS):
                split(i)
            norm_squares(1)
            norm_high(1, V_NF0)
            for f in range(FT):
                a.wait_ge(s_fh, f + 1)
                if f >= 2:
                    a.wait_ge(s_fa, f - 1)
                act_f(sl[:, f % 2, :], ps[:, f % 4, 0:T], ACT.Silu).then_inc(s_fs, 1)
                split(f + PAIRS)
                a.wait_ge(s_fa, f + 1)
                act_f(hTh[:, f, :], a32[:, f % 2, :], ACT.Copy).then_inc(s_fah, 1)
            for i in range(U_W2 + PAIRS, U_Q + PAIRS - 1):
                split(i)

            norm_squares(2)
            a.dma_start(tab, tabs).then_inc(s_tab, 16)
            norm_high(2, V_NM1)
            for i in range(U_Q + PAIRS - 1, U_V + PAIRS):
                split(i)
            for j in rjobs:
                kind, i, who = j
                bank = ps[:, rnum[j[:2]] % 8, :]
                if kind == "o":
                    a.wait_ge(s_rj, rnum[j[:2]] + 1)
                    if i >= 1:
                        a.wait_ge(s_oss, i)
                    act_f(osq, bank, ACT.Square, accum_out=rss[:, i:i + 1]).then_inc(s_oss, 1)
                    if i == 7:
                        a.wait_ge(s_om, 1)
                        act_f(rsd, rss, ACT.Sqrt).then_inc(s_or, 1)
                elif kind in "vg":
                    if i % 2 == 0:
                        u0 = (U_V if kind == "v" else U_G) + i
                        split(u0 + PAIRS)
                        split(u0 + 1 + PAIRS)
                    a.wait_ge(s_rj, rnum[j[:2]] + 1)
                    dst = vtok if kind == "v" else og
                    act_f(dst[:, i % 2, (i // 2) * 512:(i // 2 + 1) * 512], bank,
                          ACT.Copy if kind == "v" else ACT.Silu).then_inc(s_rA, 1)
                elif kind == "t":
                    t, kg = i // 4, i % 4
                    a.wait_ge(s_rj, rnum[j[:2]] + 1)
                    act_f(ogTh[:, 4 * kg:4 * kg + 4, t * P:(t + 1) * P], bank.rearrange("p (k s) -> p k s", k=4),
                          ACT.Copy).then_inc(s_rA, 1)
            for i in range(U_O + PAIRS, PRE):
                split(i)

            norm_squares(3)
            a.dma_start(gfin, rows[2:3, :].to_broadcast([P, D])).then_inc(s_gf, 16)
            norm_gain(3, V_NF1, uT3)
            a.wait_ge(s_dt, 1)
            act_f(rw(48, 2), rw(44, 2), ACT.Exp).then_inc(s_de, 1)
            a.wait_ge(s_tabr, 1)
            extras = a.value_load(itab[0:1, 0:1], min_val=0, max_val=EXTRA)
            a.wait_ge(s_pu, PRE)

            def gathered_high(before):
                for g in range(2):
                    a.wait_ge(s_xg, before + g + 1)
                    for q in range(4):
                        k = 4 * g + q
                        ins = act_f(xeTh[:, k, :], ps[:, 2 + g, q * P:(q + 1) * P], ACT.Copy, scale=vec(V_NF1, k))
                    ins.then_inc(s_xh, 1)

            def store_output(items):
                a.wait_ge(s_pu, items * E_UNITS + PRE)
                act_f(ysb[:, 0:512], ps[:, 4, :], ACT.Copy)
                act_f(ysb[:, 512:1024], ps[:, 5, :], ACT.Copy).then_inc(s_ye, 1)

            gathered_high(0)
            with a.Fori(0, extras + NE) as e:
                def split_e(lo, hi):
                    for n in range(lo, hi):
                        i = PRE + n
                        a.wait_ge(s_w[i % RING], e * (16 * E_UNITS // RING) + 16 * (i // RING + 1))
                        a.wait_ge(s_pu, e * E_UNITS + (i - M_PAIRS + 1))
                        act_f(pair(i)[0], unit(i), ACT.Copy).then_inc(s_hi, 1)

                def act_high(i):
                    a.wait_ge(s_gp, e * SMALL + (N_ACT + i))
                    act_f(actTh[:, i % 2], ps[:, 6 + i % 2, :].rearrange("p (g s) -> p g s", g=4),
                          ACT.Copy).then_inc(s_ga, 1)

                split_e(0, 4)
                store_output(e)
                split_e(4, M_PAIRS)
                for j in range(FJ):
                    u, end = first_unit(j) + M_PAIRS, min(first_unit(j + 1) + M_PAIRS, E_UNITS)
                    split_e(u, u + 1)
                    if j:
                        act_high(j - 1)
                    split_e(u + 1, u + 2)
                    a.wait_ge(s_w1, e * FJ + (j + 1))
                    if j >= 2:
                        a.wait_ge(s_ma, e * FJ + (j - 1))
                    act_f(s1[:, j % 2, :], ps[:, 2 * (j % 2), :], ACT.Silu).then_inc(s_m1, 1)
                    split_e(u + 2, end)
                act_high(FJ - 1)
                gathered_high(e * 2 + 2)
            store_output(extras + NE)
            a.wait_ge(s_gd, (extras + NE) * SMALL + 4)
            for t in range(TT):
                if t:
                    a.wait_ge(s_ss, 9)
                act_f(junk, hv[:, t, :], ACT.Square, accum_out=ss[:, 8 + t:9 + t]).then_inc(s_ss, 1)
            a.wait_ge(s_ms, 5)
            act_f(sd[:, 8:10], rstd[:, 8:10], ACT.Sqrt).then_inc(s_sd, 1)

        @block.vector
        def _(v):
            chain = [0]
            V = nc.vector

            def link(ins):
                chain[0] += 1
                ins.then_inc(d_step, 1)
                v.wait_ge(d_step, chain[0])

            def rsqrt(m, r, t):
                link(V.reciprocal(r, r))
                link(V.tensor_tensor(t, r, r, ALU.mult))
                link(V.tensor_tensor(t, t, m, ALU.mult))
                link(V.tensor_scalar(t, t, -0.5, 1.5, ALU.mult, ALU.add))
                link(V.tensor_tensor(r, r, t, ALU.mult))

            def norm_scale(n, dst):
                m = rstd[:, 2 * n:2 * n + 2]
                r = sd[:, 2 * n:2 * n + 2]
                v.wait_ge(s_ss, 2 * n + 2)
                V.tensor_scalar(m, ss[:, 2 * n:2 * n + 2], 1.0 / D, EPS, ALU.mult, ALU.add).then_inc(s_ms, 1)
                v.wait_ge(s_sd, n + 1)
                rsqrt(m, r, small[:, 184:186])
                for t in range(TT):
                    V.tensor_scalar(dst[:, t, :], hv[:, t, :], r[:, t:t + 1], None, ALU.mult).then_inc(s_xn, 1)

            def norm_gain(n, vn, dst):
                v.wait_ge(s_nt, 4 * (n + 1))
                for k in (2, 3, 6, 7):
                    V.tensor_scalar(dst[:, k, :], ps[:, k // 2, (k % 2) * T:(k % 2 + 1) * T], vec(vn, k), None,
                                    ALU.mult).then_inc(s_uTd, 1)

            def norm_low(n, vn):
                for k in range(KT):
                    v.wait_ge(s_uTa, 4 + 8 * (n - 1) + 2 * (k // 2) + 2)
                    V.scalar_tensor_tensor(out=uTl[:, k, :], in0=ps[:, k // 2, (k % 2) * T:(k % 2 + 1) * T],
                                           scalar=vec(vn, k), in1=uTh[:, k, :].bitcast(F32), op0=ALU.mult,
                                           op1=ALU.subtract).then_inc(s_uTd, 1)

            def split(i):
                v.wait_ge(s_hi, i + 1)
                V.tensor_tensor(pair(i)[1], unit(i), pair(i)[0].bitcast(F32), ALU.subtract).then_inc(s_lo, 1)

            def add_to_h(n):
                for q in range(4):
                    v.wait_ge(s_acc, 4 * n + q + 1)
                    c, t = q // 2, q % 2
                    dst = hv[:, t, c * 512:(c + 1) * 512]
                    V.tensor_tensor(dst, dst, ps[:, 4 + q, :], ALU.add).then_inc(s_h, 1)
                v.wait_ge(s_h, 4 * n + 4)

            v.wait_ge(s_c, 32)
            v.wait_ge(s_x, 16)
            norm_scale(0, xn0)
            norm_gain(0, V_NM0, uT_r)
            v.wait_ge(s_uTd, 4)
            v.wait_ge(s_uTa, 4)
            link(V.tensor_tensor(dxT[:, :, 1:T], uT_r[:, :, 0:T - 1], uT_r[:, :, 1:T], ALU.subtract))
            link(V.tensor_scalar(dxT[:, :, 0:1], uT_r[:, :, 0:1], -1.0, None, ALU.mult))
            for m, row in enumerate((1, 4, 5, 2, 0, 3)):
                if m >= 2:
                    v.wait_ge(s_pj, (1, 1, 2, J_K + 4)[m - 2])
                for k in range(KT):
                    ins = V.scalar_tensor_tensor(out=mix[m % 2][:, k, :], in0=dxT[:, k, :], scalar=vec(V_MU + row, k),
                                                 in1=uT_r[:, k, :], op0=ALU.mult, op1=ALU.add)
                ins.then_inc(s_mix, 1)
                if m == 3:
                    v.wait_ge(s_d, 1)
                    v.wait_ge(s_pz, 2)
                    d0 = dT.rearrange("p (c t) -> p c t", t=CH)[:, :, 0:1]
                    link(V.tensor_copy(d1T.rearrange("p (c t) -> p c t", t=CH)[:, :, 0:1], d0))
                    link(V.memset(d0, 0.0))
                    V.tensor_tensor_scan(gT, dT, d1T, 0.0, ALU.mult, ALU.add).then_inc(s_g, 1)
                    v.wait_ge(s_g, 1)
                    V.reciprocal(giT, gT)
                    V.tensor_copy(gC.unsqueeze(2), gT.rearrange("p (c t) -> p c t", t=CH)[:, :, CH - 1:CH])
                    for k in range(KT):
                        ins = V.tensor_scalar(fm(kmT)[:, k, :], fm(aT)[:, k, :], 1.0, vec(V_KA, k),
                                              ALU.subtract, ALU.mult)
                    link(ins)
            v.wait_ge(s_pe, J_K + 4)
            for k in range(KT):
                ins = V.tensor_scalar(fm(kkT)[:, k, :], fm(kT)[:, k, :], vec(V_KK, k), None, ALU.mult)
            ins.then_inc(s_kkr, 1)
            V.scalar_tensor_tensor(out=kmT, in0=kmT, scalar=1.0, in1=kT, op0=ALU.add, op1=ALU.mult).then_inc(s_kkr, 1)
            v.wait_ge(s_pe, J_SS + 4)
            link(V.tensor_scalar(sqT, sqT, 1e-12, None, ALU.max))
            link(V.reciprocal(sqT, sqT))
            link(V.tensor_tensor(kkT, kkT, sqT, ALU.mult))
            link(V.tensor_tensor(aT, kkT, aT, ALU.mult))
            c4 = lambda z: z.rearrange("p (n c t) -> p n c t", n=NP, c=NC)
            v.wait_ge(s_mix, 6)
            for o in range(2):
                for pos, src in ((o, kmT), (1 - o, aT)):
                    V.tensor_tensor(BK[:, :, o::2, pos, :], c4(src)[:, :, o::2, :], c4(giT)[:, :, o::2, :],
                                    ALU.mult).then_inc(s_BK, 1)
            c3 = lambda z: z.rearrange("p (c t) -> p c t", t=CH)
            A3 = AR.rearrange("p n c x t -> p (n c) x t")
            V.scalar_tensor_tensor(out=A3[:, :, 0, 1:CH], in0=c3(kkT)[:, :, 1:CH], scalar=-1.0,
                                   in1=c3(gT)[:, :, 0:CH - 1], op0=ALU.mult, op1=ALU.mult).then_inc(s_AR, 1)
            V.tensor_scalar(A3[:, :, 0, 0:1], c3(kkT)[:, :, 0:1], -1.0, None, ALU.mult).then_inc(s_AR, 1)
            V.tensor_tensor(A3[:, :, 1, :], c3(rT), c3(gT), ALU.mult).then_inc(s_AR, 1)
            v.wait_ge(s_AR, 3)
            for k in range(KT):
                ins = V.scalar_tensor_tensor(out=fm(rT)[:, k, :], in0=fm(rT)[:, k, :], scalar=vec(V_RK, k),
                                             in1=fm(kmT)[:, k, :], op0=ALU.mult, op1=ALU.mult)
            ins.then_inc(s_z, 1)
            v.wait_ge(s_BK, 4)
            V.tensor_tensor(BKh.rearrange("p n c k -> p (n c) k"), BK.rearrange("p n c x t -> p (n c) (x t)"),
                            gC.unsqueeze(2).to_broadcast([P, 32, P]), ALU.mult).then_inc(s_BKh, 1)

            v.wait_ge(s_q, 48)
            lev = lambda n, up: qc[:, Q_LEV + 128 * n + 64 * up:Q_LEV + 128 * n + 64 * up + 64]
            for j in jobs:
                kind, c, n = j
                bank = ps[:, number[j] % 8, :]
                s = sets[c % 2]
                b3 = bank.rearrange("p (n s) -> p n s", n=NP)
                if stored_by(j) == "d":
                    v.wait_ge(*made(j))
                if kind == "Z":
                    V.tensor_copy(bon.rearrange("p t h -> p (t h)"), bank[:, 0:32]).then_inc(s_jd, 1)
                elif kind == "Q":
                    par_, half = n // 2, n % 2
                    if n == 0 and c >= 2:
                        v.wait_ge(*made(("Y", c - 2, 1)))
                    V.tensor_tensor(Qm[c % 2][:, 8 * half + par_:8 * half + 8:2, :],
                                    bank.rearrange("p (h t) -> p h t", h=4),
                                    qc[:, Q_MASK:Q_MASK + P].unsqueeze(1).to_broadcast([P, 4, P]),
                                    ALU.mult).then_inc(s_jd, 1)
                elif kind == "M":
                    i, up = n % 2, n // 2
                    r = slice(64 * i, 64 * i + 64)
                    if n == 0:
                        v.wait_ge(s_zset, 2 + 2 * (c % 2))
                        if c >= 2:
                            v.wait_ge(*made(("U", c - 2, 1)))
                    mk = qc[r, (Q_MU if up else Q_ML):(Q_MU if up else Q_ML) + 64]
                    V.tensor_tensor(s["bdMT" if up else "bdM"][r, :, r], b3[r],
                                    mk.unsqueeze(1).to_broadcast([64, NP, 64]), ALU.mult).then_inc(s_jd, 1)
                    if n == 3:
                        v.wait_ge(s_jd, count[j])
                        eye = qc[:, Q_EYE:Q_EYE + 64]
                        for src, dst, up in (("bdM", "T", 0), ("bdMT", "TT", 1)):
                            for i in range(2):
                                r = slice(64 * i, 64 * i + 64)
                                ins = V.tensor_tensor(s[dst][r], s[src][r, :, r],
                                                      lev(0, up)[r].unsqueeze(1).to_broadcast([64, NP, 64]), ALU.mult)
                        link(ins)
                        for dst in ("T", "TT"):
                            ins = V.tensor_tensor(s[dst], s[dst], eye.unsqueeze(1).to_broadcast([P, NP, 64]), ALU.add)
                        ins.then_inc(s_T0, 1)
                elif kind in ("W", "WT"):
                    V.tensor_tensor(s[kind], b3, lev(n, int(kind == "WT")).unsqueeze(1).to_broadcast([P, NP, 64]),
                                    ALU.mult).then_inc(s_jd, 1)
                elif kind in ("T", "TT"):
                    if kind == "T" and n == 1:
                        v.wait_ge(s_T0, first_merges.index(c) + 1)
                    v.wait_ge(s_bd, bd_count(c, n - 1))
                    V.tensor_tensor(s[kind], s[kind], b3, ALU.add).then_inc(s_jd, 1)
                elif kind == "X":
                    v.wait_ge(*stored(("P", c, 0)))
                    V.tensor_tensor(Xst, Xst, b3, ALU.add).then_inc(s_jd, 1)
                elif kind == "U" and n == 1:
                    up = 64 * (1 - c % 2)
                    V.tensor_copy(UV[up:up + 64, c, 8:16, :].rearrange("p h v -> p (h v)"),
                                  bank[up:up + 64, :]).then_inc(s_jd, 1)
                elif kind == "S":
                    new, old = bdS[(c + 1) % 2], bdS[c % 2]
                    if c == 0:
                        v.wait_ge(s_zset, 5)
                    else:
                        v.wait_ge(*made(("Y", c - 1, 1)))
                    for i in range(2):
                        r = slice(64 * i, 64 * i + 64)
                        if c == 0:
                            ins = V.tensor_copy(new[r, :, r], b3[r])
                        else:
                            g = gC.rearrange("p (n c) -> p n c", c=NC)[r, :, c:c + 1].to_broadcast([64, NP, 64])
                            link(V.tensor_tensor(new[r, :, r], old[r, :, r], g, ALU.mult))
                            ins = V.tensor_tensor(new[r, :, r], new[r, :, r], b3[r], ALU.add)
                    ins.then_inc(s_jd, 1)
                if kind == "Y" and n == 1 and c % 2:
                    t = c // 2
                    y = yS[:, t]
                    tmp = UV[:, 0]
                    bc = lambda z: z.unsqueeze(2).to_broadcast([P, NH, HN])
                    v.wait_ge(*stored(j))
                    link(V.tensor_reduce(gsum, y, AX.X, ALU.add))
                    link(V.tensor_scalar(gsum, gsum, 1.0 / HN, None, ALU.mult))
                    link(V.tensor_tensor(y, y, bc(gsum), ALU.subtract))
                    link(V.tensor_tensor(tmp, y, y, ALU.mult))
                    link(V.tensor_reduce(gvar, tmp, AX.X, ALU.add))
                    V.tensor_scalar(gvar, gvar, 1.0 / HN, GN_EPS, ALU.mult, ALU.add).then_inc(s_gv, 1)
                    v.wait_ge(s_gs, t + 1)
                    rsqrt(gvar, gsd, gsum)
                    link(V.tensor_tensor(y, y, bc(gsd), ALU.mult))
                    v.wait_ge(s_cb, 2)
                    yf = y.rearrange("p h v -> p (h v)")
                    link(V.tensor_tensor(yf, yf, gtok[:, t, :], ALU.mult))
                    V.tensor_tensor(yf, yf, vtok_r[:, t, :], ALU.add).then_inc(s_yg, 1)
            for i in range(PAIRS):
                split(i)
            add_to_h(0)

            norm_scale(1, xn_)
            norm_low(1, V_NF0)
            for f in range(FT):
                v.wait_ge(s_fs, f + 1)
                if f >= 2:
                    v.wait_ge(s_fal, f - 1)
                V.tensor_tensor(a32[:, f % 2, :], sl[:, f % 2, :], ps[:, f % 4, T:2 * T], ALU.mult).then_inc(s_fa, 1)
                split(f + PAIRS)
                v.wait_ge(s_fah, f + 1)
                V.tensor_tensor(hTl[:, f, :], a32[:, f % 2, :], hTh[:, f, :].bitcast(F32),
                                ALU.subtract).then_inc(s_fal, 1)
            for i in range(U_W2 + PAIRS, U_Q + PAIRS - 1):
                split(i)
            add_to_h(1)

            norm_scale(2, xn_)
            norm_low(2, V_NM1)
            split(U_Q + PAIRS - 1)
            v.wait_ge(s_tab, 16)
            both = lambda a: tab[:, a:a + T].unsqueeze(1).to_broadcast([P, 2, T])
            for j in rjobs:
                kind, i, who = j
                bank = ps[:, rnum[j[:2]] % 8, :]
                if kind in "vg" and i % 2 == 0:
                    u0 = (U_V if kind == "v" else U_G) + i
                    split(u0 + PAIRS)
                    split(u0 + 1 + PAIRS)
                if who != "d":
                    continue
                v.wait_ge(s_rj, rnum[j[:2]] + 1)
                if kind in "qk":
                    dst = qTr if kind == "q" else kTr
                    b2 = bank.rearrange("p (x t) -> p x t", x=2)
                    if rcount[j[:2]] > 1:
                        v.wait_ge(s_rd, rcount[j[:2]] - 1)
                    V.tensor_tensor(rot[:, 0], b2, both(0), ALU.mult)
                    link(V.tensor_tensor(rot[:, 1], b2, both(T), ALU.mult))
                    V.tensor_tensor(dst[:, i, 0, :], rot[:, 0, 0, :], rot[:, 1, 1, :], ALU.subtract)
                    V.tensor_tensor(dst[:, i, 1, :], rot[:, 0, 1, :], rot[:, 1, 0, :], ALU.add).then_inc(s_rd, 1)
                    split((U_Q if kind == "q" else U_K) + i + PAIRS)
                elif kind == "s":
                    V.tensor_tensor(ST[:, i, :], bank[:, 0:384], tab[:, 2 * T + 384 * i:2 * T + 384 * (i + 1)],
                                    ALU.mult).then_inc(s_rd, 1)
                elif kind == "o":
                    hd, t = i // 2, i % 2
                    if i == 0:
                        v.wait_ge(s_oss, 8)
                        V.tensor_scalar(rss, rss, 1.0 / RV, EPS, ALU.mult, ALU.add).then_inc(s_om, 1)
                        v.wait_ge(s_om, 1)
                        v.wait_ge(s_or, 1)
                        rsqrt(rss, rsd, rrs)
                        v.wait_ge(*rstored(("g", 7)))
                    dst = og[:, t, hd * RV:(hd + 1) * RV]
                    V.scalar_tensor_tensor(out=dst, in0=bank, scalar=rsd[:, i:i + 1], in1=dst, op0=ALU.mult,
                                           op1=ALU.mult).then_inc(s_rd, 1)
                else:
                    t, kg = i // 4, i % 4
                    to = slice(t * P, (t + 1) * P)
                    v.wait_ge(s_rA, rstores_a + i + 1)
                    V.tensor_tensor(ogTl[:, 4 * kg:4 * kg + 4, to], bank.rearrange("p (k s) -> p k s", k=4),
                                    ogTh[:, 4 * kg:4 * kg + 4, to].bitcast(F32), ALU.subtract).then_inc(s_rd, 1)
            for i in range(U_O + PAIRS, PRE):
                split(i)
            add_to_h(2)
            V.memset(ps[:, 4:6, :], 0.0)
            V.memset(ohT, 0.0)

            norm_scale(3, xn_)
            norm_gain(3, V_NF1, uT3)
            v.wait_ge(s_lg, 1)
            lg = rw(0, 16).rearrange("p (t e) -> p t e", t=TT)
            link(V.tensor_copy(rw(0, 16), ps[:, 7, 0:16]))
            big = rw(64, 128).rearrange("p (x f) -> p x f", f=NE)
            big4 = rw(64, 128).rearrange("p (t e f) -> p t e f", t=TT, e=NE)
            eq = rw(192, 128).rearrange("p (t e f) -> p t e f", t=TT, e=NE)
            rank = rw(16, 16)
            tie = cst[:, C_TIE:C_TIE + 64].rearrange("p (e f) -> p e f", e=NE)
            for t in range(TT):
                mine = lg[:, t, :].unsqueeze(2).to_broadcast([P, NE, NE])
                other = lg[:, t, :].unsqueeze(1).to_broadcast([P, NE, NE])
                V.tensor_tensor(big4[:, t], other, mine, ALU.is_gt)
                link(V.tensor_tensor(eq[:, t], other, mine, ALU.is_equal))
                link(V.tensor_tensor(eq[:, t], eq[:, t], tie, ALU.mult))
            link(V.tensor_tensor(rw(64, 128), rw(64, 128), rw(192, 128), ALU.add))
            link(V.tensor_reduce(rank, big, AX.X, ALU.add))
            is0, is1 = rw(64, 16), rw(80, 16)
            V.tensor_scalar(is0, rank, 0.0, None, ALU.is_equal)
            link(V.tensor_scalar(is1, rank, 1.0, None, ALU.is_equal))
            mask = rw(96, 16)
            V.tensor_tensor(mask, is0, is1, ALU.add).then_inc(s_ms2, 1)
            lgf = rw(0, 16)
            pick = rw(112, 32)
            V.tensor_tensor(rw(112, 16), lgf, is0, ALU.mult)
            link(V.tensor_tensor(rw(128, 16), lgf, is1, ALU.mult))
            link(V.tensor_reduce(rw(40, 4), pick.rearrange("p (x e) -> p x e", e=NE), AX.X, ALU.add))
            V.tensor_tensor(rw(44, 2), rw(42, 2), rw(40, 2), ALU.subtract).then_inc(s_dt, 1)
            v.wait_ge(s_de, 1)
            link(V.tensor_scalar(rw(50, 2), rw(48, 2), 1.0, None, ALU.add))
            link(V.reciprocal(rw(50, 2), rw(50, 2)))
            link(V.tensor_tensor(rw(52, 2), rw(48, 2), rw(50, 2), ALU.mult))
            for t in range(TT):
                V.tensor_scalar(rw(64 + 8 * t, 8), rw(64 + 8 * t, 8), rw(50 + t, 1), None, ALU.mult)
                ins = V.tensor_scalar(rw(80 + 8 * t, 8), rw(80 + 8 * t, 8), rw(52 + t, 1), None, ALU.mult)
            link(ins)
            keys = rw(192, TT * (NI + 1)).rearrange("p (t i) -> p t i", t=TT)
            gates = rw(224, TT * (NI + 1)).rearrange("p (t i) -> p t i", t=TT)
            V.memset(keys[:, :, NI:NI + 1], 0.0)
            V.memset(gates[:, :, NI:NI + 1], 0.0)
            m3 = mask.rearrange("p (t e) -> p t e", t=TT)
            V.tensor_tensor(gates[:, :, 0:NE], is0.rearrange("p (t e) -> p t e", t=TT),
                            is1.rearrange("p (t e) -> p t e", t=TT), ALU.add)
            v.wait_ge(s_cum, 1)
            V.tensor_tensor(keys[:, :, 0:NE], m3, ps[:, 7, 32:48].rearrange("p (t e) -> p t e", t=TT), ALU.mult)
            over, order = rw(256, NE), rw(264, NE)
            link(V.tensor_scalar(over, ps[:, 7, 48:56], float(P), None, ALU.is_gt))
            link(V.tensor_tensor_scan(order, ones[:, 0:NE], over, 0.0, ALU.mult, ALU.add))
            selx = rw(272, EXTRA * NE).rearrange("p (n e) -> p n e", n=EXTRA)
            for n in range(EXTRA):
                link(V.tensor_scalar(selx[:, n, :], order, float(n + 1), None, ALU.is_equal))
                link(V.tensor_tensor(selx[:, n, :], selx[:, n, :], over, ALU.mult))
            tmp = rw(112, TT * EXTRA * NE)
            tmp4 = tmp.rearrange("p (t n e) -> p t n e", t=TT, n=EXTRA)
            for src, dst in ((keys, keys), (gates, gates)):
                for t in range(TT):
                    for n in range(EXTRA):
                        ins = V.tensor_tensor(tmp4[:, t, n, :], src[:, t, 0:NE], selx[:, n, :], ALU.mult)
                link(ins)
                link(V.tensor_reduce(dst[:, :, NE:NI], tmp4, AX.X, ALU.add))
            link(V.tensor_scalar(keys[:, :, NE:NI], keys[:, :, NE:NI], float(P), None, ALU.subtract))
            tab4 = rw(304, 4)
            V.tensor_copy(tab4[:, 0:1], order[:, NE - 1:NE])
            for n in range(EXTRA):
                ins = V.tensor_tensor(tmp4[:, 0, n, :], cst[:, C_EIDX:C_EIDX + NE], selx[:, n, :], ALU.mult)
            link(ins)
            link(V.tensor_reduce(tab4[:, 1:4], tmp4[:, 0], AX.X, ALU.add))
            V.tensor_copy(itab[:, 0:4], tab4).then_inc(s_tabr, 1)
            v.wait_ge(s_tabr, 1)
            extras = v.value_load(itab[0:1, 0:1], min_val=0, max_val=EXTRA)

            def gathered_low(before):
                for g in range(2):
                    v.wait_ge(s_xh, before + g + 1)
                    for q in range(4):
                        k = 4 * g + q
                        ins = V.scalar_tensor_tensor(out=xeTl[:, k, :], in0=ps[:, 2 + g, q * P:(q + 1) * P],
                                                     scalar=vec(V_NF1, k), in1=xeTh[:, k, :].bitcast(F32),
                                                     op0=ALU.mult, op1=ALU.subtract)
                    ins.then_inc(s_xl, 1)

            def add_back(done):
                for q in range(4):
                    v.wait_ge(s_gp, done + (q + 1))
                    t, c = q // 2, q % 2
                    dst = hv[:, t, c * 512:(c + 1) * 512]
                    V.tensor_tensor(dst, dst, ps[:, BACK[q], :], ALU.add).then_inc(s_gd, 1)

            def one_hot(item, column):
                for t in range(TT):
                    V.tensor_copy(small[:, 192 + t:193 + t], column(192 + (NI + 1) * t))
                    ins = V.tensor_copy(small[:, 194 + t:195 + t], column(224 + (NI + 1) * t))
                ins.then_inc(s_key, 1)
                v.wait_ge(s_key, item + 1)
                for t in range(TT):
                    V.tensor_scalar(oh[:, t, :], cst[:, C_IOTA:C_IOTA + P], small[:, 192 + t:193 + t], None,
                                    ALU.is_equal)
                    ins = V.tensor_scalar(ohg[:, t, :], cst[:, C_IOTA:C_IOTA + P], small[:, 192 + t:193 + t],
                                          small[:, 194 + t:195 + t], ALU.is_equal, ALU.mult)
                ins.then_inc(s_oh, 1)

            one_hot(0, lambda at: route[:, at:at + 1])
            gathered_low(0)
            with v.Fori(0, extras + NE) as e:
                def split_e(lo, hi):
                    for n in range(lo, hi):
                        i = PRE + n
                        v.wait_ge(s_hi, e * E_UNITS + (i + 1))
                        V.tensor_tensor(pair(i)[1], unit(i), pair(i)[0].bitcast(F32), ALU.subtract).then_inc(s_lo, 1)

                def act_low(i):
                    v.wait_ge(s_ga, e * FJ + (i + 1))
                    V.tensor_tensor(actTl[:, i % 2], ps[:, 6 + i % 2, :].rearrange("p (g s) -> p g s", g=4),
                                    actTh[:, i % 2].bitcast(F32), ALU.subtract).then_inc(s_gd, 1)

                split_e(0, M_PAIRS)
                for j in range(FJ):
                    u, end = first_unit(j) + M_PAIRS, min(first_unit(j + 1) + M_PAIRS, E_UNITS)
                    split_e(u, u + 1)
                    if j == 1:
                        v.wait_ge(s_gp, e * SMALL + N_OT)
                        V.tensor_copy(ohT, ps[:, 7, 0:T]).then_inc(s_gd, 1)
                    if j == 2:
                        one_hot(e + 1, lambda at: route[:, bass.ds(e + (at + 1), 1)])
                    if j:
                        act_low(j - 1)
                    split_e(u + 1, min(u + 3, end))
                    v.wait_ge(s_m1, e * FJ + (j + 1))
                    v.wait_ge(s_w3, e * FJ + (j + 1))
                    V.tensor_tensor(act[:, j % 2, :], s1[:, j % 2, :], ps[:, 2 * (j % 2) + 1, :],
                                    ALU.mult).then_inc(s_ma, 1)
                    if j == 0:
                        add_back(e * SMALL)
                    split_e(u + 3, end)
                act_low(FJ - 1)
                gathered_low(e * 2 + 2)
                v.wait_ge(s_gd, (e + 1) * SMALL)
            add_back((extras + NE) * SMALL)
            v.wait_ge(s_gd, (extras + NE) * SMALL + 4)
            norm_scale(4, xn_)
            v.wait_ge(s_xn, 10)
            v.wait_ge(s_gf, 16)
            for t in range(TT):
                V.tensor_tensor(xn_[:, t, :], xn_[:, t, :], gfin, ALU.mult).then_inc(s_fin, 1)

        @block.tensor
        def _(pe):
            owed = []

            def M(*args, **kw):
                ins = nc.tensor.matmul(*args, **kw)
                if owed:
                    ins.then_inc(owed.pop(), 1)
                return ins

            def transposes(n):
                xn = xn_ if n else xn0
                pe.wait_ge(s_xn, 2 * n + 2)
                for q in range(4):
                    for k in (2 * q, 2 * q + 1):
                        for t in range(TT):
                            ins = nc.tensor.transpose(ps[:, q, (k % 2) * T + t * P:(k % 2) * T + (t + 1) * P],
                                                      xn[:, t, k * P:(k + 1) * P], ident)
                            if owed:
                                ins.then_inc(owed.pop(), 1)
                    ins.then_inc(s_nt, 1)

            def u_ready(n):
                pe.wait_ge(s_uTa, (4, 12, 20, 24)[n])
                pe.wait_ge(s_uTd, (4, 12, 20, 24)[n])

            def M3(dst, left, right, start, stop, **kw):
                M(dst, left[0], right[0], start=start, stop=False, **kw)
                M(dst, left[0], right[1], start=False, stop=False, **kw)
                return M(dst, left[1], right[0], start=False, stop=stop, **kw)

            def parts(hl, *index):
                return tuple(z[(slice(None),) + index] for z in hl)

            pe.wait_ge(s_c, 32)
            transposes(0)

            def job(j):
                if j >= 8:
                    pe.wait_ge(s_pe, j - 7)
                return ps[:, j % 8, :]

            def arrived(i):
                pe.wait_ge(s_ra[i % 2], 16 * (i // 2 + 1))
                return slot(i % 2)

            u_ready(0)
            wa = arrived(0)
            l1 = wa[:, 0:KT * 288].rearrange("p (k n) -> p k n", k=KT)
            l2 = wa[:, KT * 288:KT * 288 + D]
            b = job(J_T1)
            for m in range(2):
                pe.wait_ge(s_mix, m + 1)
                for k in range(KT):
                    ins = M(b[64 * m:64 * m + 64, 0:T], l1[:, k, 64 * m:64 * m + 64], mix[m][:, k, :],
                            start=(k == 0), stop=(k == KT - 1))
            ins.then_inc(s_pj, 1)
            b = job(J_G1)
            pe.wait_ge(s_mix, 3)
            for lo, n, dst in ((128, 128, b[:, 0:T]), (256, 32, b[0:32, T:2 * T])):
                for k in range(KT):
                    ins = M(dst, l1[:, k, lo:lo + n], mix[0][:, k, :], start=(k == 0), stop=(k == KT - 1))
            ins.then_inc(s_pj, 1)
            pe.wait_ge(s_pe, 1)
            for base, r in ((J_W, slice(0, 64)), (J_A, slice(64, 128))):
                for q in range(4):
                    b = job(base + q)
                    for k in (2 * q, 2 * q + 1):
                        ins = M(b[:, (k % 2) * T:(k % 2 + 1) * T], l2[r, k * P:(k + 1) * P], lor[r, :],
                                start=True, stop=True)
                    ins.then_inc(s_pj, 1)
            wb = arrived(1)
            pe.wait_ge(s_pe, 2)
            for q in range(4):
                b, t, n = job(J_G + q), q % 2, q // 2
                M(b, sg1[:, t * P:(t + 1) * P], wb[:, n * 512:(n + 1) * 512], start=True, stop=False)
                M(b, sg2[:, t * P:(t + 1) * P], wb[0:32, D + n * 512:D + (n + 1) * 512], start=False,
                  stop=True).then_inc(s_pj, 1)
            for base, m, i0 in ((J_K, 3, 2), (J_R, 4, 4)):
                pe.wait_ge(s_mix, m + 1)
                for q in range(4):
                    b = job(base + q)
                    w = arrived(i0 + q // 2).rearrange("p (k n) -> p k n", k=KT)
                    for i in range(2):
                        f = 2 * (q % 2) + i
                        for k in range(KT):
                            ins = M(b[:, i * T:(i + 1) * T], w[:, k, f * P:(f + 1) * P], mix[m % 2][:, k, :],
                                    start=(k == 0), stop=(k == KT - 1))
                    ins.then_inc(s_pj, 1)
            pe.wait_ge(s_sq, 1)
            pe.wait_ge(s_q, 48)
            for q in range(4):
                M(job(J_SS + q), qc[:, Q_BO:Q_BO + P], sqT[:, q * 512:(q + 1) * 512], start=True,
                  stop=True).then_inc(s_pj, 1)
            pe.wait_ge(s_mix, 6)
            for q in range(4):
                b, t, n = job(J_V + q), q % 2, q // 2
                w = arrived(6 + n).rearrange("p (k n) -> p k n", k=KT)
                for k in range(KT):
                    ins = M(b, mix[1][:, k, t * P:(t + 1) * P], w[:, k, :], start=(k == 0), stop=(k == KT - 1))
                ins.then_inc(s_pj, 1)

            pe.wait_ge(s_pe, J_V + 4)
            pe.wait_ge(s_uv, NC)
            for j in jobs:
                kind, c, n = j
                i = number[j]
                bank = ps[:, i % 8, :]
                s = sets[c % 2]
                if i >= 8:
                    if jobs[i - 8][0] == "G":
                        pe.wait_ge(s_ygT, jobs[i - 8][1] + 1)
                    else:
                        pe.wait_ge(*stored(jobs[i - 8]))
                if kind == "B":
                    if c == 0:
                        pe.wait_ge(s_BKh, 1)
                    for x_ in range(NC):
                        ins = nc.tensor.transpose(bank[:, x_ * P:(x_ + 1) * P], BKh[:, c, x_, :], ident)
                elif kind == "Z":
                    pe.wait_ge(s_z, 1)
                    for t in range(TT):
                        for p_ in range(NP):
                            ins = M(bank[:, 16 * t + 2 * p_:16 * t + 2 * p_ + 2], fm(rT)[:, p_, t * P:(t + 1) * P],
                                    qc[:, Q_SEL:Q_SEL + 2], start=True, stop=True)
                elif kind == "Q":
                    r = slice(64 * (n // 2), 64 * (n // 2) + 64)
                    for q in range(4):
                        p_ = 4 * (n % 2) + q
                        ins = M(bank[:, q * P:(q + 1) * P], BK[r, p_, c].rearrange("p x t -> p (x t)"),
                                AR[r, p_, c].rearrange("p x t -> p (x t)"), start=True, stop=True)
                elif kind == "M":
                    r = slice(64 * (n % 2), 64 * (n % 2) + 64)
                    for p_ in range(NP):
                        A_, B_ = AR[r, p_, c, 0, :], BK[r, p_, c, 1 - c % 2, :]
                        ins = M(bank[r, p_ * 64:(p_ + 1) * 64], *((A_, B_) if n < 2 else (B_, A_)),
                                start=True, stop=True)
                elif kind in ("W", "WT", "T", "TT"):
                    lhs = {"W": "bdMT", "WT": "bdM", "T": "bdTT", "TT": "bdT"}[kind]
                    rhs = {"W": "T", "WT": "TT", "T": "W", "TT": "WT"}[kind]
                    if kind in ("W", "WT"):
                        if n == 1:
                            pe.wait_ge(*stored(("M", c, 3)))
                            pe.wait_ge(s_T0, first_merges.index(c) + 1)
                        else:
                            pe.wait_ge(*stored((rhs, c, n - 1)))
                    else:
                        pe.wait_ge(s_bd, bd_count(c, n - 1))
                        pe.wait_ge(*stored((rhs, c, n)))
                    for p_ in range(NP):
                        ins = M(bank[:, p_ * 64:(p_ + 1) * 64], s[lhs][:, p_, :], s[rhs][:, p_, :],
                                start=True, stop=True)
                elif kind == "P":
                    pe.wait_ge(*stored(("Q", c, 3)))
                    for hd in range(NH):
                        r, p_ = 64 * (hd % 2), hd // 2
                        ins = M(bank[r:r + 64, p_ * 64:(p_ + 1) * 64], Qm[c % 2][:, hd, 0:64], UV[:, c, hd, :],
                                start=True, stop=True)
                elif kind == "X":
                    pe.wait_ge(*stored(("S", c - 1, 0)))
                    for hd in range(NH):
                        r, p_ = 64 * (hd % 2), hd // 2
                        ins = M(bank[r:r + 64, p_ * 64:(p_ + 1) * 64], AR[:, p_, c, 0, :],
                                bdS[c % 2][:, p_, r:r + 64], start=True, stop=True)
                elif kind == "U":
                    up = 64 * (1 - c % 2)
                    if n == 0:
                        pe.wait_ge(s_bd, bd_count(c, LEVELS - 1))
                        pe.wait_ge(*stored(("X" if c else "P", c, 0)))
                    for q in range(8):
                        hd = 8 * n + q
                        ins = M(bank[up:up + 64, q * 64:(q + 1) * 64],
                                s["bdTT"][:, hd // 2, 64 * (hd % 2):64 * (hd % 2) + 64], Xst[:, hd // 2, :],
                                start=True, stop=True)
                elif kind == "S":
                    pe.wait_ge(*stored(("U", c, 0)))
                    pe.wait_ge(*stored(("U", c, 1)))
                    for hd in range(NH):
                        r, p_ = 64 * (hd % 2), hd // 2
                        ins = M(bank[r:r + 64, p_ * 64:(p_ + 1) * 64], BKT[:, p_, c, r:r + 64], UV[:, c, hd, :],
                                start=True, stop=True)
                elif kind == "Y":
                    if c == NC - 1:
                        pe.wait_ge(*stored(("U", c, 0)))
                        pe.wait_ge(*stored(("U", c, 1)))
                    r0 = 64 * (c % 2)
                    for q in range(4):
                        p_ = 4 * n + q
                        if c > 0:
                            M(bank[r0:r0 + 64, q * P:(q + 1) * P], AR[:, p_, c, 1, :], bdS[c % 2][:, p_, :],
                              start=True, stop=False, skip_group_check=True)
                        for i2 in range(2):
                            ins = M(bank[r0:r0 + 64, q * P + 64 * i2:q * P + 64 * i2 + 64],
                                    Qm[c % 2][:, 2 * p_ + i2, 64:128], UV[:, c, 2 * p_ + i2, :],
                                    start=(c == 0), stop=True, skip_group_check=True)
                elif kind == "G":
                    t, half = c // 2, c % 2
                    pe.wait_ge(s_yg, t + 1)
                    yf = yS[:, t].rearrange("p h v -> p (h v)")
                    for q in range(4):
                        k = 4 * half + q
                        ins = nc.tensor.transpose(bank[:, q * P:(q + 1) * P], yf[:, k * P:(k + 1) * P], ident)
                ins.then_inc(s_job, 1)
            pe.wait_ge(s_ygT, 4)
            for q in range(4):
                c, t = q // 2, q % 2
                w = arrived(8 + c).rearrange("p (k n) -> p k n", k=KT)
                for k in range(KT):
                    ins = M(ps[:, 4 + q, :], ygT[:, k, t * P:(t + 1) * P], w[:, k, :], start=(k == 0),
                            stop=(k == KT - 1))
                ins.then_inc(s_acc, 1)

            def split_unit(i, dims, **sizes):
                pe.wait_ge(s_lo, i + 1)
                return tuple(z.rearrange(f"p ({dims}) -> p {dims}", **sizes) for z in pair(i))

            transposes(1)
            u_ready(1)
            uT_ = (uTh, uTl)
            for f in range(FT):
                w = split_unit(f, "k g n", k=KT, g=2)
                if f >= 4:
                    pe.wait_ge(s_fa, f - 3)
                for i in range(2):
                    for k in range(KT):
                        ins = M3(ps[:, f % 4, i * T:(i + 1) * T], parts(w, k, i), parts(uT_, k),
                                 start=(k == 0), stop=(k == KT - 1))
                ins.then_inc(s_fh, 1)
                owed.append(s_pu)
            for f in range(FT):
                if f % 2 == 0:
                    w = split_unit(U_W2 + f // 2, "g n", g=2)
                pe.wait_ge(s_fal, f + 1)
                for q in range(4):
                    c, t = q // 2, q % 2
                    ins = M3(ps[:, 4 + q, :], parts((hTh, hTl), f, slice(t * P, (t + 1) * P)),
                             parts(w, f % 2, slice(c * 512, (c + 1) * 512)),
                             start=(f == 0), stop=(f == FT - 1), skip_group_check=True)
                    if f == FT - 1:
                        ins.then_inc(s_acc, 1)
                if f == FT - 1:
                    owed.append(s_pu)
                elif f % 2:
                    ins.then_inc(s_pu, 1)

            transposes(2)
            u_ready(2)
            for j in rjobs:
                kind, i, who = j
                n = rnum[j[:2]]
                bank = ps[:, n % 8, :]
                if n >= 8:
                    pe.wait_ge(*rstored(rjobs[n - 8][:2]))
                if kind in "qk":
                    w = split_unit((U_Q if kind == "q" else U_K) + i, "k y n", k=KT, y=2)
                    for y in range(2):
                        for k in range(KT):
                            ins = M3(bank[:, y * T:(y + 1) * T], parts(w, k, y), parts(uT_, k),
                                     start=(k == 0), stop=(k == KT - 1))
                    owed.append(s_pu)
                elif kind in "vg":
                    if i % 2:
                        ins = None
                    else:
                        u0 = (U_V if kind == "v" else U_G) + i
                        pe.wait_ge(*rstored(rjobs[n - 7][:2]))
                        for half in range(2):
                            w = split_unit(u0 + half, "k n", k=4)
                            for t in range(TT):
                                for q in range(4):
                                    k = 4 * half + q
                                    ins = M3(ps[:, (n + t) % 8, :], parts(uT_, k, slice(t * P, (t + 1) * P)),
                                             parts(w, q), start=(k == 0), stop=(k == KT - 1))
                                if half:
                                    ins.then_inc(s_rj, 1)
                                elif t:
                                    ins.then_inc(s_pu, 1)
                        owed.append(s_pu)
                        ins = None
                elif kind == "s":
                    pe.wait_ge(*rstored(("k", i)))
                    for y in range(2):
                        M(bank[:, 0:256], kTr[:, i, y, 0:P], qTr[:, i, y, :], start=(y == 0), stop=(y == 1))
                    for y in range(2):
                        ins = M(bank[:, 256:384], kTr[:, i, y, P:T], qTr[:, i, y, P:T], start=(y == 0), stop=(y == 1))
                elif kind == "o":
                    hd, t = i // 2, i % 2
                    if i == 0:
                        pe.wait_ge(*rstored(("s", RH - 1)))
                        pe.wait_ge(*rstored(("v", 7)))
                    for c in range(2):
                        cs = slice(c * 256, (c + 1) * 256)
                        vs = slice(hd * RV + c * 256, hd * RV + (c + 1) * 256)
                        ins = M(bank[:, cs], ST[:, hd, t * P:(t + 1) * P], vtok[:, 0, vs], start=True, stop=(t == 0))
                        if t:
                            ins = M(bank[:, cs], ST[:, hd, 256:384], vtok[:, 1, vs], start=False, stop=True)
                else:
                    t, kg = i // 4, i % 4
                    if i == 0:
                        pe.wait_ge(*rstored(("o", 7)))
                    for q in range(4):
                        k = 4 * kg + q
                        ins = nc.tensor.transpose(bank[:, q * P:(q + 1) * P], og[:, t, k * P:(k + 1) * P], ident)
                if ins is not None:
                    ins.then_inc(s_rj, 1)
            pe.wait_ge(*rstored(("t", 7)))
            for k in range(16):
                if k % 2 == 0:
                    w = split_unit(U_O + k // 2, "g n", g=2)
                for q in range(4):
                    c, t = q // 2, q % 2
                    ins = M3(ps[:, 4 + q, :], parts((ogTh, ogTl), k, slice(t * P, (t + 1) * P)),
                             parts(w, k % 2, slice(c * 512, (c + 1) * 512)),
                             start=(k == 0), stop=(k == 15), skip_group_check=True)
                    if k == 15:
                        ins.then_inc(s_acc, 1)
                if k == 15:
                    owed.append(s_pu)
                elif k % 2:
                    ins.then_inc(s_pu, 1)

            transposes(3)
            u_ready(3)
            for t in range(TT):
                for k in range(KT):
                    ins = M(ps[:, 7, 8 * t:8 * t + 8], uT3[:, k, t * P:(t + 1) * P],
                            par[:, P_ROUTER + 8 * k:P_ROUTER + 8 * k + 8], start=(k == 0), stop=(k == KT - 1))
            ins.then_inc(s_lg, 1)
            pe.wait_ge(s_ms2, 1)
            tri = cst[:, C_TRI:C_TRI + P]
            m0, m1 = rw(96, 8), rw(104, 8)
            M(ps[:, 7, 32:40], tri, m0, start=True, stop=True)
            M(ps[:, 7, 40:48], ones, m0, start=True, stop=False)
            M(ps[:, 7, 40:48], tri, m1, start=False, stop=True)
            M(ps[:, 7, 48:56], ones, m0, start=True, stop=False)
            M(ps[:, 7, 48:56], ones, m1, start=False, stop=True).then_inc(s_cum, 1)

            def gather(item):
                pe.wait_ge(s_oh, item + 1)
                for g in range(2):
                    for q in range(4):
                        k = 4 * g + q
                        for t in range(TT):
                            ins = M(ps[:, 2 + g, q * P:(q + 1) * P], xn_[:, t, k * P:(k + 1) * P], oh[:, t, :],
                                    start=(t == 0), stop=(t == TT - 1))
                    ins.then_inc(s_xg, 1)

            def send_back(item):
                pe.wait_ge(s_ye, item + 1)
                for q in range(4):
                    t, c = q // 2, q % 2
                    for i in range(2):
                        ins = M(ps[:, BACK[q], i * 256:(i + 1) * 256], ohT[:, t * P:(t + 1) * P],
                                ysb[:, c * 512 + i * 256:c * 512 + (i + 1) * 256], start=True, stop=True)
                    ins.then_inc(s_gp, 1)

            gather(0)
            extras = pe.value_load(itab[0:1, 0:1], min_val=0, max_val=EXTRA)
            with pe.Fori(0, extras + NE) as e:
                def units(n, dims, **sizes):
                    pe.wait_ge(s_lo, e * E_UNITS + (PRE + n + 1))
                    return tuple(z.rearrange(f"p ({dims}) -> p {dims}", **sizes) for z in pair(PRE + n))

                def hidden(j, i, done):
                    for half in range(2):
                        w = units(first_unit(j) + 2 * i + half, "k n", k=4)
                        for q in range(4):
                            k = 4 * half + q
                            ins = M3(ps[:, 2 * (j % 2) + i, :], parts((xeTh, xeTl), k), parts(w, q),
                                     start=(k == 0), stop=(k == KT - 1))
                        if half == 0:
                            ins.then_inc(s_pu, 1)
                    ins.then_inc(done, 1)
                    owed.append(s_pu)

                def transpose_act(i):
                    pe.wait_ge(s_ma, e * FJ + (i + 1))
                    pe.wait_ge(s_gd, e * SMALL + (N_ACT + i - 2 if i else 2))
                    for g in range(4):
                        ins = nc.tensor.transpose(ps[:, 6 + i % 2, g * P:(g + 1) * P],
                                                  act[:, i % 2, g * P:(g + 1) * P], ident)
                        if owed:
                            ins.then_inc(owed.pop(), 1)
                    ins.then_inc(s_gp, 1)

                def output(i):
                    pe.wait_ge(s_gd, e * SMALL + (N_ACT + i))
                    for half in range(2):
                        w = units(first_unit(i + 1) + 4 * (i < FJ - 1) + half, "g n", g=2)
                        for g in range(2):
                            for c in range(2):
                                ins = M3(ps[:, 4 + c, :], parts((actTh, actTl), i % 2, 2 * half + g),
                                         parts(w, g, slice(c * 512, (c + 1) * 512)),
                                         start=(i == 0 and half == 0 and g == 0),
                                         stop=(i == FJ - 1 and half == 1 and g == 1), skip_group_check=True)
                        ins.then_inc(s_pu, 1)

                pe.wait_ge(s_xl, e * 2 + 2)
                for j in range(FJ):
                    if j >= 2:
                        pe.wait_ge(s_ma, e * FJ + (j - 1))
                    hidden(j, 0, s_w1)
                    if j == 1:
                        pe.wait_ge(s_gd, e * SMALL + 1)
                        for t in range(TT):
                            ins = nc.tensor.transpose(ps[:, 7, t * P:(t + 1) * P], ohg[:, t, :], ident)
                            if owed:
                                ins.then_inc(owed.pop(), 1)
                        ins.then_inc(s_gp, 1)
                    if j:
                        transpose_act(j - 1)
                    hidden(j, 1, s_w3)
                    if j == 0:
                        send_back(e)
                    else:
                        output(j - 1)
                transpose_act(FJ - 1)
                gather(e + 1)
                output(FJ - 1)
            send_back(extras + NE)


def kernel(**inputs):
    import concourse.bacc as _bacc
    from concourse.bass_utils import run_bass_kernel_spmd as _run

    g = {k: np.asarray(v) for k, v in inputs.items()}

    def cols(w, n=512):
        k_, n_ = w.shape
        return w.reshape(k_ // P, P, n_ // n, n).transpose(2, 1, 0, 3).reshape(n_ // n, P, k_ // P * n)

    def halves(w):
        return cols(w).reshape(-1, P, 2, UNIT).transpose(0, 2, 1, 3).reshape(-1, P, UNIT)

    def rows_of(w):
        return w.reshape(-1, 2, P, D).transpose(0, 2, 1, 3).reshape(-1, P, 2 * D)

    lora = np.zeros((2, P, SLOT), np.float32)
    first = np.concatenate([g["a_w1"][0], g["a_a1"][0], g["a_g1"][0]], axis=1)
    lora[0, :, :KT * 288] = cols(first, 288)[0]
    lora[0, :64, KT * 288:KT * 288 + D] = g["a_w2"][0]
    lora[0, 64:, KT * 288:KT * 288 + D] = g["a_a2"][0]
    lora[1, :, :D] = g["a_g2"][0, :P]
    lora[1, :32, D:2 * D] = g["a_g2"][0, P:]
    rstream = np.concatenate([lora] + [cols(g[n][0]) for n in ("a_wk", "a_wr", "a_wv", "a_wo")])
    w13 = np.stack([g[n][0].reshape(KT, P, FT, P) for n in ("f_w1", "f_w3")], axis=3)
    w13 = w13.transpose(2, 1, 0, 3, 4).reshape(FT, P, UNIT)

    def parity(w):
        return w.reshape(D, RH, RK // 2, 2).transpose(0, 1, 3, 2).reshape(D, D)

    pstream = np.concatenate([w13, rows_of(g["f_w2"][0]), cols(parity(g["b_wq"][0]), RK),
                              cols(parity(g["b_wk"][0]), RK), halves(g["b_wv"][0]), halves(g["b_wg"][0]),
                              rows_of(g["b_wo"][0])])
    mstream = np.empty((NE, 3 * FJ, 2, P, UNIT), np.float32)
    at1 = [0, 2] + [5 + 3 * i for i in range(FJ - 2)]
    at2 = [4 + 3 * i for i in range(FJ - 1)] + [3 * FJ - 1]
    for e in range(NE):
        mstream[e, at1] = halves(g["m_w1"][0, e]).reshape(FJ, 2, P, UNIT)
        mstream[e, [i + 1 for i in at1]] = halves(g["m_w3"][0, e]).reshape(FJ, 2, P, UNIT)
        mstream[e, at2] = rows_of(g["m_w2"][0, e]).reshape(FJ, 2, P, UNIT)
    mstream = mstream.reshape(NE * E_UNITS, P, UNIT)

    vecs = np.concatenate([g["norm_mix"][0:1], g["norm_ffn"][0:1], g["norm_mix"][1:2], g["norm_ffn"][1:2],
                           g["a_mu"][0], g["a_w0"], g["a_a0"], g["a_kk"], g["a_ka"], g["a_rk"].reshape(1, D)])
    params = np.concatenate([vecs.reshape(15, KT, P).transpose(2, 0, 1).reshape(P, 15 * KT),
                             g["m_router"][0].reshape(KT, P, NE).transpose(1, 0, 2).reshape(P, KT * NE)], axis=1)
    rows = np.concatenate([g["a_gn_w"], g["a_gn_b"], g["norm_final"][None]])
    consts, qconsts, tabs = const_tables()
    arrays = {"x": g["x"].reshape(TT, P, D).transpose(1, 0, 2), "consts": consts, "qconsts": qconsts, "tabs": tabs,
              "params": params, "rows": rows, "rstream": rstream, "pstream": pstream, "mstream": mstream}
    arrays = {k: np.ascontiguousarray(v) for k, v in arrays.items()}
    nc = _bacc.Bacc("TRN2", target_bir_lowering=False, num_devices=1)
    aps = [nc.dram_tensor(k, v.shape, mybir.dt.from_np(v.dtype), kind="ExternalInput").ap() for k, v in arrays.items()]
    out = nc.dram_tensor("out", (P, TT, D), F32, kind="ExternalOutput").ap()
    build(nc, *aps, out)
    r = _run(nc, [arrays], core_ids=[0])
    return r.results[0]["out"].reshape(P, TT, D).transpose(1, 0, 2).reshape(1, T, D)
```
